# Optimizing a Trainium2 kernel written in Bass

```python
import math
import jax, jax.numpy as jnp
from jax import lax
import numpy as np

D_MODEL = 1024
BATCH = 1
SEQ = 512
DEPTH = 1

N_META = 16
BLOCK = 128
PAD = BLOCK - N_META
CHUNK = 64
HG_HEADS = D_MODEL // 128
HG_DK = 128
HG_DV = 128
HG_KDIM = HG_HEADS * HG_DK
HG_WIDTH = HG_HEADS * HG_DV
DA_HEADS = D_MODEL // 128
DA_D = 64
DA_WIDTH = DA_HEADS * 2 * DA_D
ROPE_DIM = DA_D // 4
ROPE_THETA = 500000.0
EPS = 1e-6
PROJ_SIZES = (HG_KDIM, HG_KDIM, HG_WIDTH, HG_WIDTH,
              DA_WIDTH, DA_WIDTH, DA_WIDTH, DA_WIDTH, D_MODEL, D_MODEL)
PROJ_WIDTH = sum(PROJ_SIZES)

kernel_name = "hgrn2_diffattn_gated_hybrid"

def rmsnorm(x, g):
    xf = x.astype(jnp.float32)
    y = xf * lax.rsqrt(jnp.mean(xf * xf, axis=-1, keepdims=True) + EPS)
    return (y * g.astype(jnp.float32)).astype(x.dtype)

def split_heads(a, n_heads):
    b, l, w = a.shape
    return a.reshape(b, l, n_heads, w // n_heads).transpose(0, 2, 1, 3)

def merge_heads(a):
    b, h, l, dh = a.shape
    return a.transpose(0, 2, 1, 3).reshape(b, l, h * dh)

def rope_partial(x, pos):
    half = ROPE_DIM // 2
    inv = ROPE_THETA ** (-jnp.arange(half, dtype=jnp.float32) * 2.0 / ROPE_DIM)
    ang = pos.astype(jnp.float32)[:, None] * inv[None, :]
    cos = jnp.cos(ang).astype(x.dtype)
    sin = jnp.sin(ang).astype(x.dtype)
    x1, x2, xp = x[..., :half], x[..., half:ROPE_DIM], x[..., ROPE_DIM:]
    return jnp.concatenate([x1 * cos - x2 * sin, x2 * cos + x1 * sin, xp], axis=-1)

def hgrn2_chunked(q, logf, k, v):
    B, H, L, DK = q.shape
    DV = v.shape[-1]
    n = L // CHUNK

    def to_chunks(a):
        return a.reshape(B, H, n, CHUNK, a.shape[-1]).transpose(2, 0, 1, 3, 4)

    causal = jnp.tril(jnp.ones((CHUNK, CHUNK), dtype=bool))[None, None, :, :, None]

    def step(S, inp):
        qb, gb, kb, vb = inp
        b = jnp.cumsum(gb, axis=2)
        rel = b[:, :, :, None, :] - b[:, :, None, :, :]
        dec = jnp.where(causal, jnp.exp(jnp.minimum(rel, 0.0)), 0.0)
        A = jnp.einsum('bhtd,bhsd,bhtsd->bhts', qb, kb, dec)
        o = (jnp.einsum('bhts,bhsv->bhtv', A, vb)
             + jnp.einsum('bhtd,bhdv->bhtv', qb * jnp.exp(b), S))
        bl = b[:, :, -1:, :]
        S_new = (jnp.exp(bl[:, :, 0, :])[..., None] * S
                 + jnp.einsum('bhsd,bhsv->bhdv', kb * jnp.exp(bl - b), vb))
        return S_new, o

    S0 = jnp.zeros((B, H, DK, DV), jnp.float32)
    _, oc = lax.scan(step, S0, (to_chunks(q), to_chunks(logf), to_chunks(k), to_chunks(v)))
    return oc.transpose(1, 2, 0, 3, 4).reshape(B, H, L, DV)

def diff_attention(q1, k1, q2, k2, v, lam):
    L = q1.shape[2]
    d = q1.shape[-1]
    n = L // BLOCK
    scale = d ** -0.5
    key_idx = jnp.arange(L)
    valid_key = key_idx >= PAD

    def block(i):
        s0 = i * BLOCK
        qb1 = lax.dynamic_slice_in_dim(q1, s0, BLOCK, axis=2)
        qb2 = lax.dynamic_slice_in_dim(q2, s0, BLOCK, axis=2)
        qidx = s0 + jnp.arange(BLOCK)
        mask = valid_key[None, :] & (key_idx[None, :] <= qidx[:, None])

        def probs(qb, kk):
            s = jnp.einsum('bhqd,bhkd->bhqk', qb, kk).astype(jnp.float32) * scale
            return jax.nn.softmax(jnp.where(mask, s, -1e30), axis=-1)

        p = probs(qb1, k1) - lam * probs(qb2, k2)
        return jnp.einsum('bhqk,bhkv->bhqv', p.astype(v.dtype), v)

    out = lax.map(block, jnp.arange(n))
    B, H = q1.shape[0], q1.shape[1]
    return out.transpose(1, 2, 0, 3, 4).reshape(B, H, L, v.shape[-1])

def setup_inputs(seed: int = 0) -> dict:
    key = jax.random.key(seed)
    ks = jax.random.split(key, 14)
    f32 = jnp.float32
    nrm = lambda k, shape, s: jax.random.normal(k, shape, f32) * s
    return {
        "x": nrm(ks[0], (BATCH, SEQ, D_MODEL), 1.0),
        "meta_tokens": nrm(ks[1], (N_META, D_MODEL), 1.0),
        "norm_g": 1.0 + nrm(ks[2], (DEPTH, D_MODEL), 0.02),
        "w_in": nrm(ks[3], (DEPTH, D_MODEL, PROJ_WIDTH), D_MODEL ** -0.5),
        "hg_lb_logits": nrm(ks[4], (DEPTH + 1, HG_KDIM), 0.5),
        "hg_norm_g": 1.0 + nrm(ks[5], (DEPTH, HG_DV), 0.02),
        "da_lambda": nrm(ks[6], (DEPTH, 4, DA_D), 0.1),
        "da_norm_g": 1.0 + nrm(ks[7], (DEPTH, 2 * DA_D), 0.02),
        "w_branch_a": nrm(ks[8], (DEPTH, HG_WIDTH, D_MODEL), HG_WIDTH ** -0.5),
        "w_branch_b": nrm(ks[9], (DEPTH, DA_WIDTH, D_MODEL), DA_WIDTH ** -0.5),
        "w_out": nrm(ks[10], (DEPTH, D_MODEL, D_MODEL), D_MODEL ** -0.5),
        "final_g": 1.0 + nrm(ks[11], (D_MODEL,), 0.02),
    }

def reference(x, meta_tokens, norm_g, w_in, hg_lb_logits, hg_norm_g, da_lambda,
              da_norm_g, w_branch_a, w_branch_b, w_out, final_g):
    B, S, D = x.shape
    dt = x.dtype
    h = jnp.concatenate([jnp.zeros((B, PAD, D), dt),
                         jnp.broadcast_to(meta_tokens.astype(dt)[None], (B, N_META, D)),
                         x], axis=1)
    Lp = h.shape[1]
    idx = jnp.arange(Lp)
    valid = idx >= PAD
    pos = jnp.maximum(idx - PAD, 0)
    offs = [int(o) for o in np.cumsum(PROJ_SIZES)[:-1]]
    lb_all = jnp.cumsum(jax.nn.softmax(hg_lb_logits.astype(jnp.float32), axis=0), axis=0)

    for l in range(DEPTH):
        u = rmsnorm(h, norm_g[l])
        proj = jnp.einsum('bld,de->ble', u, w_in[l])
        hq, hf, hi, hz, aq, ak, av, az, ga, gb = jnp.split(proj, offs, axis=-1)

        lb = lb_all[l]
        f = lb + (1.0 - lb) * jax.nn.sigmoid(hf.astype(jnp.float32))
        f = jnp.where(valid[None, :, None], f, 1.0)
        kA = 1.0 - f
        oA = hgrn2_chunked(split_heads(hq.astype(jnp.float32), HG_HEADS),
                           split_heads(jnp.log(f), HG_HEADS),
                           split_heads(kA, HG_HEADS),
                           split_heads(hi.astype(jnp.float32), HG_HEADS))
        oA = merge_heads(rmsnorm(oA.astype(dt), hg_norm_g[l]))
        yA = jnp.einsum('blw,wd->bld', oA * jax.nn.silu(hz), w_branch_a[l])

        lam_init = 0.8 - 0.6 * math.exp(-0.3 * l)
        lp = da_lambda[l].astype(jnp.float32)
        lam = jnp.exp(jnp.sum(lp[0] * lp[1])) - jnp.exp(jnp.sum(lp[2] * lp[3])) + lam_init
        qh = split_heads(aq, DA_HEADS)
        kh = split_heads(ak, DA_HEADS)
        vh = split_heads(av, DA_HEADS)
        q1 = rope_partial(qh[..., :DA_D], pos)
        q2 = rope_partial(qh[..., DA_D:], pos)
        k1 = rope_partial(kh[..., :DA_D], pos)
        k2 = rope_partial(kh[..., DA_D:], pos)
        oB = diff_attention(q1, k1, q2, k2, vh, lam)
        oB = merge_heads(rmsnorm(oB, da_norm_g[l]) * (1.0 - lam_init))
        yB = jnp.einsum('blw,wd->bld', oB * jax.nn.silu(az), w_branch_b[l])

        m = jax.nn.sigmoid(ga) * yA + jax.nn.sigmoid(gb) * yB
        h = h + jnp.einsum('bld,de->ble', m, w_out[l])

    out = rmsnorm(h, final_g)
    return out[:, PAD + N_META:, :]


_drawn_inputs = setup_inputs


def setup_inputs(seed=0):
    import zlib

    import numpy as np

    out = dict(_drawn_inputs(seed))
    spreads = {}
    factors = {'norm_g': 3.44, 'hg_norm_g': 8.0, 'da_norm_g': 8.0, 'final_g': 2.827}
    for name, (base, spread) in spreads.items():
        noise = np.random.default_rng([zlib.crc32(name.encode()), seed]).standard_normal(out[name].shape)
        drawn = base * np.exp(spread * noise) if base else spread * noise
        out[name] = __import__('jax').numpy.asarray(drawn.astype(out[name].dtype))
    for name, factor in factors.items():
        out[name] = (out[name] * factor).astype(out[name].dtype)
    return out
```

```python
import numpy as np
import concourse.bass as bass
from concourse import mybir

F32 = mybir.dt.float32
F32R = mybir.dt.float32r
BF16 = mybir.dt.bfloat16
U32 = mybir.dt.uint32
ALU = mybir.AluOpType
ACT = mybir.ActivationFunctionType
AX = mybir.AxisListType

P = 128
D = 1024
SEQ = 512
META = 16
TOK = META + SEQ
KT = D // P
HEADS = D // P
CH = SEQ // P
NT = CH + 1
EPS = 1e-6
LAM_INIT = 0.2
DA_D = 64
SCALE = DA_D ** -0.5
ROPE_DIM = DA_D // 4
ROPE_THETA = 500000.0
NEG = -1e30
LEVELS = [1 << i for i in range(7)]
MASKED = 6
HQ, HF, HI, HZ, AQ, AK, AV, AZ, GA, GB = (i * D for i in range(10))

UNIT = 1024
V_UNITS = 16
H_UNITS = 6 * HEADS
T_UNITS = 4 * KT
O_UNITS = 8
H0 = V_UNITS
T0 = H0 + H_UNITS
O0 = T0 + T_UNITS
ALL_UNITS = O0 + O_UNITS

HG = 12
AT = 4 * CH + 1


def constants():
    ident = np.eye(P, dtype=np.float32)
    q, k = np.arange(P)[:, None], np.arange(P)[None, :]
    bias = np.where(k <= q, np.float32(0), np.float32(NEG)).astype(np.float32)
    masks = np.zeros((P, MASKED, P // 2), np.uint32)
    s = np.arange(P)[:, None]
    j = np.arange(P // 2)[None, :]
    for i, m in enumerate(LEVELS[:MASKED]):
        t = (j // m) * 2 * m + m + j % m
        masks[:, i, :] = (s // (2 * m) == t // (2 * m)) & (s % (2 * m) < m)
    half = ROPE_DIM // 2
    inv = np.float32(ROPE_THETA) ** (-np.arange(half, dtype=np.float32) * np.float32(2.0) / np.float32(ROPE_DIM))
    ang = np.arange(TOK, dtype=np.float32)[None, :] * inv.astype(np.float32)[:, None]
    cos, sin = np.cos(ang), np.sin(ang)
    rope = np.zeros((P, 2, TOK), np.float32)
    rope[:, 0, :] = 1.0
    for c in (0, DA_D):
        rope[c:c + half, 0], rope[c + half:c + ROPE_DIM, 0] = cos, cos
        rope[c:c + half, 1], rope[c + half:c + ROPE_DIM, 1] = -sin, sin
    return {"c_ident": ident, "c_bias": bias, "c_masks": masks, "c_rope": rope}


def build(nc, x, meta_tokens, norm_g, w_in, lb_logits, hg_norm_g, da_lambda, da_norm_g,
          w_branch_a, w_branch_b, w_out, final_g, c_ident, c_bias, c_masks, c_rope, out):
    x = x.rearrange("b s d -> (b s) d")
    out = out.rearrange("b s d -> (b s) d")
    w_in = w_in.rearrange("l (k p) n -> p (l k) n", p=P)
    w_branch_a = w_branch_a.rearrange("l (k p) n -> p (l k) n", p=P)
    w_branch_b = w_branch_b.rearrange("l (k p) n -> p (l k) n", p=P)
    w_out = w_out.rearrange("l (k p) n -> p (l k) n", p=P)

    names = {}

    def at(name, shape, dt, offset):
        size = int(np.prod(shape[1:])) * (2 if dt == BF16 else 4)
        names[name] = nc.alloc_sbuf_tensor_at(name, shape, dt, offset=offset)
        return names[name], offset + (size + 31) // 32 * 32

    base = 16512
    uT_hi, o = at("uT_hi", [P, KT, TOK], F32R, base)
    uT_lo, o = at("uT_lo", [P, KT, TOK], F32R, o)
    w_raw, o = at("w_raw", [P, 4, UNIT], F32, o)
    w_hi, o = at("w_hi", [P, 4, UNIT], F32R, o)
    w_lo, o = at("w_lo", [P, 4, UNIT], F32R, o)
    region_g = o
    x_in, o2 = at("x_in", [P, NT, D], F32, region_g)
    g_in, o2 = at("g_in", [P, D], F32, o2)
    og_a, o = at("og_a", [P, HEADS, SEQ], F32, region_g)
    og_b, o = at("og_b", [P, HEADS, SEQ], F32, o)
    m_hi, o2 = at("m_hi", [P, KT, SEQ], F32R, region_g)
    m_lo, o2 = at("m_lo", [P, KT, SEQ], F32R, o2)
    region_v = o
    v_both, o = at("v_both", [P, 2 * NT, D], F32, region_v)
    v_a, v_b = v_both[:, 0:NT, :], v_both[:, NT:2 * NT, :]
    oa_hi, o2 = at("oa_hi", [P, KT, SEQ], F32R, region_v)
    oa_lo, o2 = at("oa_lo", [P, KT, SEQ], F32R, o2)
    ident, o = at("ident", [P, P], F32, o)
    ident_bf, o = at("ident_bf", [P, P], BF16, o)
    bias_bf, o = at("bias_bf", [P, P], BF16, o)
    masks, o = at("masks", [P, MASKED, P // 2], U32, o)
    rope, o = at("rope", [P, 2, TOK], F32, o)
    small, o = at("small", [P, 96], F32, o)
    region_w = o
    th, o = at("th", [P, TOK], F32, o)
    f, o = at("f", [P, TOK], F32, o)
    kk, o = at("kk", [P, TOK], F32, o)
    qq, o = at("qq", [P, SEQ], F32, o)
    q_raw, o = at("q_raw", [P, SEQ], F32, o)
    tt, o = at("tt", [P, TOK], F32, o)
    aa, o = at("aa", [P, CH, P], F32, o)
    k_tok, o = at("k_tok", [P, CH, P], F32, o)
    st, o = at("st", [P, CH, P], F32, o)
    sq, o = at("sq", [P, CH, P], F32, o)
    on, o = at("on", [P, CH, P], F32, o)
    th_z, o = at("th_z", [P, SEQ], F32, o)
    z_g, o = at("z_g", [P, SEQ], F32, o)
    gate_a, o = at("gate_a", [P, SEQ], F32, o)
    gate_b, o = at("gate_b", [P, SEQ], F32, o)
    ak_raw, o = at("ak_raw", [P, TOK], F32, o)
    aq_raw, o = at("aq_raw", [P, SEQ], F32, o)
    shuf, o = at("shuf", [P, TOK], F32, o)
    kT, o = at("kT", [P, TOK], F32, o)
    qT, o = at("qT", [P, SEQ], F32, o)
    e1, o = at("e1", [P, TOK], F32, o)
    e2, o = at("e2", [P, TOK], F32, o)
    pT, o = at("pT", [P, NT, P], F32, o)
    lam_in, _ = at("lam_in", [P, 4, DA_D], F32, region_w)
    rows_in, _ = at("rows_in", [2 * HEADS + 2, P], F32, region_w + 4096)
    bias_in, _ = at("bias_in", [P, P], F32, region_w + 8192)
    lam_pr, _ = at("lam_pr", [P, 2, DA_D], F32, region_w + 12288)
    x_sq, _ = at("x_sq", [P, D], F32, region_w + 16384)
    ob_hi, o2 = at("ob_hi", [P, KT, SEQ], F32R, region_w)
    ob_lo, o2 = at("ob_lo", [P, KT, SEQ], F32R, o2)
    t_gate, o2 = at("t_gate", [P, 2, SEQ], F32, o2)
    t_m, o2 = at("t_m", [P, 2, SEQ], F32, o2)
    x_sq2, _ = at("x_sq2", [P, D], F32, region_w)
    x_res, o3 = at("x_res", [P, CH, D], F32, base)
    g_fin, o3 = at("g_fin", [P, D], F32, o3)
    assert o3 <= base + 2 * KT * TOK * 4
    y_out, o3 = at("y_out", [P, CH, D], F32, region_v)

    lbt = small[:, 0:2 * HEADS + 2]
    f_mul, f_neg, f_add = (small[:, 18 + HEADS * i:26 + HEADS * i] for i in range(3))
    tmp8 = [small[:, 42 + HEADS * i:50 + HEADS * i] for i in range(3)]
    gain_a, gain_b, neg_lam = small[:, 66:67], small[:, 67:68], small[:, 68:69]
    lam2 = small[:, 70:72]
    ss, ms, rstd, half_neg = small[:, 72:77], small[:, 77:82], small[:, 82:87], small[:, 87:92]
    soft, _ = at("soft", [P, 8], F32, o)
    mx, nb, lsum, rl = soft[:, 0:2], soft[:, 2:4], soft[:, 4:6], soft[:, 6:8]

    ps = nc.alloc_psum_tensor("ps", [P, 8, 512], F32)
    pf = ps[:].rearrange("p b c -> p (b c)")

    def bank(i):
        return ps[:, i, :]

    LV = (4, 5)
    B_O, B_KT, B_G, B_OT, B_ATO = 3, 6, 7, 4, 6
    SC0 = 4 * 512

    sem = nc.alloc_semaphore
    consts_in, x_loaded, xres_loaded, stored = sem("consts_in"), sem("x_loaded"), sem("xres_loaded"), sem("stored")
    w_loaded = [sem(f"w_loaded{i}") for i in range(4)]
    slot_free = sem("slot_free")
    hi_ready, lo_ready, w_used = sem("hi_ready"), sem("lo_ready"), sem("w_used")
    v_pre, a_pre, g_pre, pe_pre = sem("v_pre"), sem("a_pre"), sem("g_pre"), sem("pe_pre")
    u_ready_hi, u_ready_lo = sem("u_ready_hi"), sem("u_ready_lo")
    x_squared, x_rstd, x_normed, x_turned = sem("x_squared"), sem("x_rstd"), sem("x_normed"), sem("x_turned")
    x_ms = sem("x_ms")
    va_taken, vd_taken = sem("va_taken"), sem("vd_taken")
    sec_taken = sem("sec_taken")
    dve_own = sem("dve_own")
    k_ready, lvl_ready, lvl_taken = sem("k_ready"), sem("lvl_ready"), sem("lvl_taken")
    hg_done, at_done = sem("hg_done"), sem("at_done")
    ktok_ready, st_ready = sem("ktok_ready"), sem("st_ready")
    o_squared, ms_ready, rstd_ready, on_ready, og_ready = (sem(n) for n in (
        "o_squared", "ms_ready", "rstd_ready", "on_ready", "og_ready"))
    rope_ready, gate_ready = sem("rope_ready"), sem("gate_ready")
    nb_ready, exp_done, p_ready, pT_ready = sem("nb_ready"), sem("exp_done"), sem("p_ready"), sem("pT_ready")
    og_hi, og_lo = sem("og_hi"), sem("og_lo")
    gate_taken, y_taken, m_sum, mhi_ready, mlo_ready = (sem(n) for n in (
        "gate_taken", "y_taken", "m_sum", "mhi_ready", "mlo_ready"))
    o_taken, o_sq, o_ms, o_rstd, y_ready, t_own = (sem(n) for n in (
        "o_taken", "o_sq", "o_ms", "o_rstd", "y_ready", "t_own"))

    def wait_loaded(eng, slot, loads):
        eng.wait_ge(w_loaded[slot], loads * 16)

    def head_loads(h, p):
        return 2 * h + 7 + p // 3

    def convert_hi(act, u, slot, loads):
        wait_loaded(act, slot, loads)
        if not isinstance(u, int) or u >= 3:
            act.wait_ge(w_used, u - 2)
        act.activation(w_hi[:, slot, :], w_raw[:, slot, :], ACT.Copy).then_inc(hi_ready, 1)

    def convert_lo(dve, u, slot):
        dve.wait_ge(hi_ready, u + 1)
        dve.tensor_tensor(w_lo[:, slot, :], w_raw[:, slot, :], w_hi[:, slot, :].bitcast(F32),
                          ALU.subtract).then_inc(lo_ready, 1)

    def hg(h, step):
        return HG * (h + 1) + step + 1

    def atn(h, step):
        return AT * (h + 1) + step + 1

    block = nc.Block()
    with block:
        @block.sync
        def _(sp):
            for i in range(CH):
                sp.dma_start(x_in[:, i, :], x[i * P:(i + 1) * P, :]).then_inc(x_loaded, 16)
            def load(u, slot, src):
                if not isinstance(u, int) or u >= 3:
                    sp.wait_ge(lo_ready, u - 2)
                    if not isinstance(u, int):
                        sp.sem_inc(slot_free, 1)
                sp.dma_start(w_raw[:, slot, :].rearrange("p (k n) -> p k n", k=src.shape[1]), src) \
                    .then_inc(w_loaded[slot], 16)

            for j in range(4):
                for c in range(4):
                    col = (HI, AV)[j // 2] + 512 * (j % 2)
                    load(4 * j + c, c, w_in[:, 2 * c:2 * c + 2, col:col + 512])

            def section(h, s, u, slot):
                col = (HF, HQ, AK, AQ, HZ, AZ)[s]
                load(u, slot, w_in[:, :, bass.ds(h * P + col, P)])

            for s in range(4):
                section(0, s, H0 + s, s % 3)
            with sp.Fori(0, HEADS - 1) as h:
                for p in range(6):
                    section(h if p < 2 else h + 1, (p + 4) % 6, H0 + 6 * h + 4 + p, (p + 1) % 3)
            for p in range(2):
                section(HEADS - 1, 4 + p, H0 + H_UNITS - 2 + p, (p + 1) % 3)
            for d in range(KT):
                cols = slice(d * P, (d + 1) * P)
                for j, src in enumerate((w_in[:, :, GA + d * P:GA + (d + 1) * P],
                                         w_in[:, :, GB + d * P:GB + (d + 1) * P],
                                         w_branch_a[:, :, cols], w_branch_b[:, :, cols])):
                    load(T0 + 4 * d + j, j, src)
            for j in range(2):
                for c in range(4):
                    load(O0 + 4 * j + c, c, w_out[:, 2 * c:2 * c + 2, 512 * j:512 * (j + 1)])
                if j == 0:
                    sp.wait_ge(w_used, T0 + T_UNITS - 2)
                    for i in range(CH):
                        sp.dma_start(x_res[:, i, :], x[i * P:(i + 1) * P, :]).then_inc(xres_loaded, 16)
                    sp.dma_start(g_fin[:, :], final_g.rearrange("(a n) -> a n", a=1).to_broadcast([P, D])) \
                        .then_inc(xres_loaded, 16)
            for i in range(CH):
                sp.wait_ge(y_ready, i + 1)
                sp.dma_start(out[i * P:(i + 1) * P, :], y_out[:, i, :]).then_inc(stored, 16)
            sp.wait_ge(stored, 16 * CH)

        @block.gpsimd
        def _(pool):
            pool.memset(ss, 1.0)
            pool.memset(half_neg, -0.5).then_inc(g_pre, 1)
            pool.dma_start(ident[:, :], c_ident).then_inc(consts_in, 16)
            pool.dma_start(x_in[0:META, CH, :], meta_tokens).then_inc(consts_in, 16)
            pool.dma_start(g_in[:, :], norm_g.to_broadcast([P, D])).then_inc(consts_in, 16)
            pool.dma_start(rows_in[0:2 * HEADS, :], lb_logits.rearrange("r (h p) -> (r h) p", p=P)) \
                .then_inc(consts_in, 16)
            pool.dma_start(rows_in[2 * HEADS:2 * HEADS + 1, :], hg_norm_g).then_inc(consts_in, 16)
            pool.dma_start(rows_in[2 * HEADS + 1:2 * HEADS + 2, :], da_norm_g).then_inc(consts_in, 16)
            pool.dma_start(lam_in[:, :, :].rearrange("p r d -> p (r d)"),
                           da_lambda.rearrange("l r d -> l (r d)").to_broadcast([P, 4 * DA_D])) \
                .then_inc(consts_in, 16)
            pool.dma_start(bias_in[:, :], c_bias).then_inc(consts_in, 16)
            pool.dma_start(masks[:, :, :], c_masks).then_inc(consts_in, 16)
            pool.dma_start(rope[:, :, :], c_rope).then_inc(consts_in, 16)

            pool.wait_ge(g_pre, 1)
            pool.wait_ge(x_ms, 1)
            pool.tensor_tensor(rstd[:, 0:NT], ms[:, 0:NT], half_neg[:, 0:NT], ALU.pow).then_inc(x_rstd, 1)
            with pool.Fori(0, 2 * HEADS) as b:
                pool.wait_ge(ms_ready, b + 1)
                pool.tensor_tensor(rstd[:, 0:CH], ms[:, 0:CH], half_neg[:, 0:CH], ALU.pow).then_inc(rstd_ready, 1)
            pool.wait_ge(o_ms, 1)
            pool.tensor_tensor(rstd[:, 0:CH], ms[:, 0:CH], half_neg[:, 0:CH], ALU.pow).then_inc(o_rstd, 1)

        @block.tensor
        def _(pe):
            def three(dst, w, rhs, start, stop):
                pe.matmul(dst, w[0], rhs[0], start=start, stop=False, skip_group_check=True)
                pe.matmul(dst, w[0], rhs[1], start=False, stop=False, skip_group_check=True)
                return pe.matmul(dst, w[1], rhs[0], start=False, stop=stop, skip_group_check=True)

            pe.wait_ge(consts_in, 160)
            pe.transpose(bank(0)[:, 0:2 * HEADS + 2], rows_in[:, :], ident[0:2 * HEADS + 2, 0:2 * HEADS + 2]) \
                .then_inc(pe_pre, 1)
            pe.wait_ge(v_pre, 1)
            for i in range(CH):
                pe.wait_ge(x_normed, i + 1)
                for k in range(KT):
                    t = pe.transpose(ps[:, 2 * i + k // 4, (k % 4) * P:(k % 4 + 1) * P],
                                     x_in[:, i, k * P:(k + 1) * P], ident[:, :])
                t.then_inc(x_turned, 1)
            pe.wait_ge(x_normed, NT)
            pe.wait_ge(u_ready_lo, 1)
            for k in range(KT):
                t = pe.transpose(bank(0)[:, k * META:(k + 1) * META], x_in[0:META, CH, k * P:(k + 1) * P],
                                 ident[0:META, 0:META])
            t.then_inc(x_turned, 1)

            pe.wait_ge(u_ready_lo, NT)
            with pe.Fori(0, 2) as jj:
                for hh in range(2):
                    for c in range(4):
                        u = 8 * jj + 4 * hh + c
                        pe.wait_ge(lo_ready, u + 1)
                        for t in range(NT):
                            dst = bank((t, (5 + t) % 8)[hh])
                            m = P if t < CH else META
                            lo = META + t * P if t < CH else 0
                            dst = dst[0:m, :]
                            if c == 0:
                                if hh == 0:
                                    if t == 0:
                                        pe.wait_ge(va_taken, 6 * jj + 1)
                                    if t == 1:
                                        pe.wait_ge(vd_taken, 4 * jj + 1)
                                else:
                                    if t == 0:
                                        pe.wait_ge(va_taken, 6 * jj + 3)
                                        pe.wait_ge(vd_taken, 4 * jj + 2)
                                    if t == 3:
                                        pe.wait_ge(va_taken, 6 * jj + 4)
                                    if t == 4:
                                        pe.wait_ge(vd_taken, 4 * jj + 3)
                            for k in range(2):
                                us = tuple(a[:, 2 * c + k, lo:lo + m] for a in (uT_hi, uT_lo))
                                ws = tuple(a[:, c, 512 * k:512 * (k + 1)] for a in (w_hi, w_lo))
                                last = three(dst, us, ws, c == 0 and k == 0, c == 3 and k == 1)
                        last.then_inc(w_used, 1)

            def groups(n, s, p_slot, ks):
                slot = p_slot
                if ks[0] == 0:
                    pe.wait_ge(lo_ready, H0 + n + 1)
                    if not isinstance(n, int) or n >= 2:
                        pe.wait_ge(sec_taken, n - 1)
                for k in ks:
                    w = tuple(a[:, slot, k * P:(k + 1) * P] for a in (w_hi, w_lo))
                    if s in (0, 2):
                        for b in range(2):
                            rhs = tuple(a[:, k, b * (TOK // 2):(b + 1) * (TOK // 2)] for a in (uT_hi, uT_lo))
                            last = three(bank(b)[:, 0:TOK // 2], w, rhs, k == 0, k == KT - 1)
                    else:
                        rhs = tuple(a[:, k, META:TOK] for a in (uT_hi, uT_lo))
                        last = three(bank(0 if s == 4 else 2), w, rhs, k == 0, k == KT - 1)
                    if k == KT - 1:
                        last.then_inc(w_used, 1)

            pe.wait_ge(va_taken, 15)
            pe.wait_ge(vd_taken, 10)
            for s in range(4):
                groups(s, s, s % 3, range(KT))

            def mixer(h):
                vcol = bass.ds(h * P, P)

                def level(e):
                    dst = bank(LV[e % 2])
                    if e <= 1:
                        if e == 0:
                            pe.wait_ge(k_ready, h + 1)
                            pe.wait_ge(og_ready, 2 * h + 2)
                    else:
                        pe.wait_ge(lvl_ready, 7 * h + e - 1)
                    if e >= 2:
                        pe.wait_ge(lvl_taken, 8 * h + e - 1)
                    for c in range(CH):
                        kc = kk[:, META + c * P:META + (c + 1) * P]
                        qc = qq[:, c * P:(c + 1) * P]
                        if e == 0:
                            mm = pe.matmul(dst[:, c * P:(c + 1) * P], kc, q_raw[:, c * P:(c + 1) * P],
                                           start=True, stop=True)
                        elif e <= MASKED:
                            m = LEVELS[e - 1]
                            second = qc.rearrange("p (b two m) -> p b two m", two=2, m=m)[:, :, 1, :]
                            o3d = dst[:, c * 64:(c + 1) * 64].rearrange("p (b m) -> p b m", m=m)
                            mm = pe.matmul(o3d, kc, second, start=True, stop=True)
                        else:
                            mm = pe.matmul(dst[0:64, c * 64:(c + 1) * 64], kc[:, 0:64], qc[:, 64:128],
                                           start=True, stop=True)
                    mm.then_inc(hg_done, 1)

                def keys_token_major():
                    pe.wait_ge(lvl_ready, 7 * h + 7)
                    for c in range(CH - 1):
                        pe.transpose(bank(B_KT)[:, c * P:(c + 1) * P],
                                     kk[:, META + c * P:META + (c + 1) * P], ident[:, :])
                    pe.transpose(bank(B_KT)[0:META, (CH - 1) * P:], kk[:, 0:META], ident[:, :]) \
                        .then_inc(hg_done, 1)

                def state_sums():
                    pe.wait_ge(ktok_ready, h + 1)
                    g = bank(B_G)
                    for c in range(CH - 1):
                        pe.matmul(g[:, (c + 1) * P:(c + 2) * P], k_tok[:, c, :], v_a[:, c, vcol],
                                  start=True, stop=True)
                    pe.matmul(g[:, 0:P], k_tok[0:META, CH - 1, :], v_a[0:META, CH, vcol], start=True, stop=True) \
                        .then_inc(hg_done, 1)

                def outputs():
                    pe.wait_ge(lvl_taken, 8 * h + 8)
                    pe.wait_ge(st_ready, h + 1)
                    for c in range(CH):
                        dst = bank(B_O)[:, c * P:(c + 1) * P]
                        pe.matmul(dst, aa[:, c, :], v_a[:, c, vcol], start=True, stop=False)
                        mm = pe.matmul(dst, qq[:, c * P:(c + 1) * P], st[:, c, :], start=False, stop=True)
                    mm.then_inc(hg_done, 1)

                def turn(branch, b, done):
                    pe.wait_ge(on_ready, 2 * h + 1 + branch)
                    for c in range(CH):
                        mm = pe.transpose(bank(b)[:, c * P:(c + 1) * P], on[:, c, :], ident[:, :])
                    mm.then_inc(done, 1)

                def scores(b, comp):
                    if b == 0 and comp == 0:
                        pe.wait_ge(rope_ready, h + 1)
                        pe.wait_ge(og_ready, 2 * h + 3)
                    else:
                        pe.wait_ge(exp_done, 8 * h + 2 * b + comp)
                    rows = slice(comp * DA_D, (comp + 1) * DA_D)
                    n = META + b * P
                    q = qT[rows, b * P:(b + 1) * P]
                    pe.matmul(pf[:, SC0 + 512 - n:SC0 + 512], q, kT[rows, 0:n], start=True, stop=True)
                    pe.matmul(pf[:, SC0 + 512:SC0 + 512 + P], q, kT[rows, n:n + P], start=True, stop=False)
                    pe.matmul(pf[:, SC0 + 512:SC0 + 512 + P], ident_bf[:, :], bias_bf[:, :],
                              start=False, stop=True).then_inc(at_done, 1)

                def turn_probs(b):
                    pe.wait_ge(p_ready, 4 * h + b + 1)
                    if b > 0:
                        pe.wait_ge(pT_ready, 4 * h + b)
                    for j in range(b + 1):
                        pe.transpose(bank(6)[:, j * P:(j + 1) * P], e1[:, META + j * P:META + (j + 1) * P],
                                     ident[:, :])
                    pe.transpose(bank(7)[0:META, 0:P], e1[:, 0:META], ident[:, :]).then_inc(at_done, 1)

                def attend(b):
                    pe.wait_ge(pT_ready, 4 * h + b + 1)
                    dst = bank(B_O)[:, b * P:(b + 1) * P]
                    for j in range(b + 1):
                        pe.matmul(dst, pT[:, j, :], v_b[:, j, vcol], start=(j == 0), stop=False)
                    pe.matmul(dst, pT[0:META, CH, :], v_b[0:META, CH, vcol], start=False, stop=True) \
                        .then_inc(at_done, 1)

                return {
                    (0, 2): lambda: (level(0), level(1)),
                    (0, 4): lambda: level(2),
                    (0, 6): lambda: level(3),
                    (1, 0): lambda: level(4),
                    (1, 2): lambda: level(5),
                    (1, 4): lambda: level(6),
                    (1, 6): lambda: level(7),
                    (2, 0): keys_token_major,
                    (2, 2): state_sums,
                    (2, 4): outputs,
                    (2, 7): lambda: turn(0, B_OT, hg_done),
                    (3, 1): lambda: scores(0, 0),
                    (3, 3): lambda: scores(0, 1),
                    (3, 5): lambda: turn_probs(0),
                    (3, 6): lambda: scores(1, 0),
                    (3, 7): lambda: attend(0),
                    (4, 0): lambda: scores(1, 1),
                    (4, 2): lambda: turn_probs(1),
                    (4, 3): lambda: scores(2, 0),
                    (4, 4): lambda: attend(1),
                    (4, 5): lambda: scores(2, 1),
                    (4, 7): lambda: turn_probs(2),
                    (5, 0): lambda: scores(3, 0),
                    (5, 1): lambda: attend(2),
                    (5, 2): lambda: scores(3, 1),
                    (5, 4): lambda: turn_probs(3),
                    (5, 6): lambda: attend(3),
                    (5, 7): lambda: turn(1, B_ATO, at_done),
                }

            def head(h, periods):
                steps = mixer(h)
                for p in range(6):
                    for g in range(KT):
                        if p < periods:
                            groups(6 * h + 4 + p, (p + 4) % 6, (p + 1) % 3, [g])
                        if (p, g) in steps:
                            steps[(p, g)]()

            with pe.Fori(0, HEADS - 1) as h:
                head(h, 6)
            head(HEADS - 1, 2)

            oa, ob = (oa_hi, oa_lo), (ob_hi, ob_lo)
            pe.wait_ge(sec_taken, H_UNITS)
            pe.wait_ge(og_ready, 2 * HEADS + 2)
            for d in range(KT):
                for j in range(4):
                    v = 4 * d + j
                    b = 4 * (d % 2) + j
                    pe.wait_ge(lo_ready, T0 + v + 1)
                    if d >= 2 and j < 2:
                        pe.wait_ge(gate_taken, 2 * (d - 2) + j + 1)
                    if d >= 2 and j >= 2:
                        pe.wait_ge(y_taken, 2 * (d - 2) + j - 1)
                    for k in range(KT):
                        w = tuple(a[:, j, k * P:(k + 1) * P] for a in (w_hi, w_lo))
                        if j < 2:
                            rhs = tuple(a[:, k, META:TOK] for a in (uT_hi, uT_lo))
                        else:
                            if d == 0:
                                pe.wait_ge(og_lo, (j - 2) * HEADS + k + 1)
                            rhs = tuple(a[:, k, :] for a in (oa, ob)[j - 2])
                        last = three(bank(b), w, rhs, k == 0, k == KT - 1)
                    last.then_inc(w_used, 1)
            for j in range(2):
                for c in range(4):
                    pe.wait_ge(lo_ready, O0 + 4 * j + c + 1)
                    if c == 0 and j == 0:
                        pe.wait_ge(y_taken, 2 * KT)
                    for t in range(CH):
                        for k in range(2):
                            if j == 0 and t == 0:
                                pe.wait_ge(mlo_ready, 2 * c + k + 1)
                            ms_ = tuple(a[:, 2 * c + k, t * P:(t + 1) * P] for a in (m_hi, m_lo))
                            ws = tuple(a[:, c, 512 * k:512 * (k + 1)] for a in (w_hi, w_lo))
                            last = three(bank(4 * j + t), ms_, ws, c == 0 and k == 0, c == 3 and k == 1)
                    last.then_inc(w_used, 1)

        @block.scalar
        def _(act):
            act.sem_inc(va_taken, 3)
            act.sem_inc(vd_taken, 2)
            act.sem_inc(og_ready, 2)
            act.sem_inc(hg_done, HG)
            act.sem_inc(at_done, AT)
            act.sem_inc(gate_ready, 2)
            act.wait_ge(g_pre, 1)
            act.wait_ge(x_loaded, 64)
            for i in range(CH):
                act.activation(x_sq[:, :], x_in[:, i, :], ACT.Square, accum_out=ss[:, i:i + 1]) \
                    .then_inc(x_squared, 1)
                act.wait_ge(x_squared, i + 1)
            act.wait_ge(consts_in, 160)
            act.activation(x_sq[0:META, :], x_in[0:META, CH, :], ACT.Square, accum_out=ss[0:META, CH:NT]) \
                .then_inc(x_squared, 1)
            convert_hi(act, 0, 0, 1)
            convert_hi(act, 1, 1, 1)
            act.wait_ge(v_pre, 4)
            act.activation(lam2, lam2, ACT.Exp).then_inc(a_pre, 1)
            act.wait_ge(v_pre, 6)
            act.activation(tmp8[0], tmp8[0], ACT.Exp).then_inc(a_pre, 1)
            act.wait_ge(v_pre, 7)
            act.activation(tmp8[1], tmp8[1], ACT.Exp).then_inc(a_pre, 1)
            for i in range(CH):
                act.wait_ge(x_turned, i + 1)
                for g in range(2):
                    ins = act.activation(uT_hi[:, 4 * g:4 * g + 4, META + i * P:META + (i + 1) * P],
                                         bank(2 * i + g).rearrange("p (k t) -> p k t", k=4), ACT.Copy)
                ins.then_inc(u_ready_hi, 1)
            act.wait_ge(x_turned, NT)
            act.activation(uT_hi[:, :, 0:META], bank(0)[:, 0:KT * META].rearrange("p (k t) -> p k t", k=KT),
                           ACT.Copy).then_inc(u_ready_hi, 1)

            with act.Fori(0, 2) as jj:
                for hh in range(2):
                    for c in range(4):
                        u = 8 * jj + 4 * hh + c + 2
                        slot = (c + 2) % 4
                        convert_hi(act, u, slot, 2 * jj + hh + (c + 2) // 4 + 1)
                    act.wait_ge(w_used, 8 * jj + 4 * hh + 4)
                    for t in ((0, 2, 4), (3, 0, 2))[hh]:
                        b = (t, (5 + t) % 8)[hh]
                        m = P if t < CH else META
                        act.activation(v_both[0:m, bass.ds(jj * NT + t, 1), hh * 512:(hh + 1) * 512].rearrange("p a n -> p (a n)"),
                                       bank(b)[0:m, :], ACT.Copy).then_inc(va_taken, 1)

            def take(h, s):
                n = 6 * h + s
                act.wait_ge(w_used, H0 + n + 1)
                if s == 0:
                    act.wait_ge(k_ready, h) if not isinstance(h, int) or h > 0 else None
                    act.activation(th[:, :].rearrange("p (b t) -> p b t", b=2), ps[:, 0:2, 0:TOK // 2], ACT.Tanh,
                                   scale=0.5).then_inc(sec_taken, 1)
                elif s == 1:
                    act.wait_ge(hg_done, hg(h - 1, 0))
                    act.activation(q_raw[:, :], bank(2), ACT.Copy).then_inc(sec_taken, 1)
                elif s in (2, 3):
                    if not isinstance(h, int) or h > 0:
                        act.wait_ge(rope_ready, h)
                    if s == 2:
                        act.activation(ak_raw[:, :].rearrange("p (b t) -> p b t", b=2), ps[:, 0:2, 0:TOK // 2],
                                       ACT.Copy).then_inc(sec_taken, 1)
                    else:
                        act.activation(aq_raw[:, :], bank(2), ACT.Copy).then_inc(sec_taken, 1)
                else:
                    src = bank(0 if s == 4 else 2)
                    act.wait_ge(gate_ready, 2 * h + s - 2 - (0))
                    act.activation(th_z[:, :], src, ACT.Tanh, scale=0.5)
                    act.activation(z_g[:, :], src, ACT.Copy, scale=(gain_a if s == 4 else gain_b)) \
                        .then_inc(sec_taken, 1)

            for n in range(4):
                convert_hi(act, H0 + n + 2, (n + 2) % 3, 4 + (n + 2) // 3 + 1)
                if n > 0:
                    take(0, n - 1)

            def square(branch, h, done, step):
                act.wait_ge(done, step)
                act.activation(sq[:, :, :].rearrange("p c d -> p (c d)"), bank(B_O), ACT.Square) \
                    .then_inc(o_squared, 1)

            def exp(h, b, comp):
                n = META + b * P
                act.wait_ge(nb_ready, 8 * h + 2 * b + comp + 1)
                if comp == 0:
                    act.wait_ge(at_done, atn(h - 1, 14) if b == 0 else atn(h, (2, 6, 10)[b - 1]))
                act.activation((e1, e2)[comp][:, 0:n + P], pf[:, SC0 + 512 - n:SC0 + 512 + P], ACT.Exp,
                               bias=nb[:, comp:comp + 1], scale=SCALE, accum_out=lsum[:, comp:comp + 1]) \
                    .then_inc(exp_done, 1)

            def probs_out(h, b):
                act.wait_ge(at_done, atn(h, (2, 6, 10, 14)[b]))
                act.activation(pT[:, 0:b + 1, :].rearrange("p j q -> p (j q)"), bank(6)[:, 0:(b + 1) * P], ACT.Copy)
                act.activation(pT[0:META, CH, :], bank(7)[0:META, 0:P], ACT.Copy).then_inc(pT_ready, 1)

            def head(h, periods):
                def conv(p):
                    if p < periods:
                        convert_hi(act, H0 + 6 * h + 6 + p, p % 3, head_loads(h, p))
                last = periods < 6
                take(h, 3)
                conv(0)
                take(h, 4)
                conv(1)
                take(h, 5)
                conv(2)
                act.wait_ge(hg_done, hg(h, 8))
                act.activation(k_tok[:, 0:CH - 1, :].rearrange("p c d -> p (c d)"), bank(B_KT)[:, 0:(CH - 1) * P],
                               ACT.Copy)
                act.activation(k_tok[0:META, CH - 1, :], bank(B_KT)[0:META, (CH - 1) * P:], ACT.Copy) \
                    .then_inc(ktok_ready, 1)
                square(0, h, hg_done, hg(h, 10))
                if not last:
                    take(h + 1, 0)
                conv(3)
                exp(h, 0, 0)
                exp(h, 0, 1)
                probs_out(h, 0)
                exp(h, 1, 0)
                if not last:
                    take(h + 1, 1)
                conv(4)
                exp(h, 1, 1)
                probs_out(h, 1)
                exp(h, 2, 0)
                exp(h, 2, 1)
                probs_out(h, 2)
                if not last:
                    take(h + 1, 2)
                conv(5)
                exp(h, 3, 0)
                exp(h, 3, 1)
                probs_out(h, 3)
                square(1, h, at_done, atn(h, 15))

            with act.Fori(0, HEADS - 1) as h:
                head(h, 6)
            head(HEADS - 1, 2)

            act.wait_ge(og_ready, 2 * HEADS + 2)
            for b, (src, dst) in enumerate(((og_a, oa_hi), (og_b, ob_hi))):
                for k in range(HEADS):
                    act.activation(dst[:, k, :], src[:, k, :], ACT.Copy).then_inc(og_hi, 1)
                    if b == 0 and k in (3, 7):
                        v = k // 4
                        convert_hi(act, T0 + v + 2, (v + 2) % 4, (20, 20, 20, 4)[(v + 2) % 4] + (v + 2) // 4 + 1)
            for v in range(T_UNITS + O_UNITS):
                d, j = v // 4, v % 4
                if 2 <= v < T_UNITS + O_UNITS - 2:
                    u = v + 2
                    convert_hi(act, T0 + u, u % 4, (20, 20, 20, 4)[u % 4] + u // 4 + 1)
                if v < T_UNITS and j < 2:
                    act.wait_ge(w_used, T0 + v + 1)
                    if d >= 1:
                        act.wait_ge(y_taken, 2 * (d - 1) + j + 1)
                    act.activation(t_gate[:, j, :], bank(4 * (d % 2) + j), ACT.Tanh, scale=0.5) \
                        .then_inc(gate_taken, 1)
                if j == 1 and 1 <= d <= KT:
                    act.wait_ge(m_sum, d)
                    act.activation(m_hi[:, d - 1, :], t_m[:, 0, :], ACT.Copy, scale=0.5).then_inc(mhi_ready, 1)
            for t in range(CH):
                act.wait_ge(o_taken, t + 1)
                act.activation(x_sq2[:, :], y_out[:, t, :], ACT.Square, accum_out=ss[:, t:t + 1]).then_inc(o_sq, 1)
                act.wait_ge(o_sq, t + 1)

        @block.vector
        def _(dve):
            own = [0]

            def pre(ins):
                own[0] += 1
                ins.then_inc(v_pre, 1)
                return own[0]

            dve.wait_ge(pe_pre, 1)
            pre(dve.tensor_copy(lbt, bank(0)[:, 0:2 * HEADS + 2]))
            dve.wait_ge(consts_in, 160)
            pre(dve.tensor_copy(bias_bf[:, :], bias_in[:, :]))
            pre(dve.tensor_tensor(lam_pr[:, :, :], lam_in[:, 0:4:2, :], lam_in[:, 1:4:2, :], ALU.mult))
            dve.wait_ge(v_pre, 3)
            pre(dve.tensor_reduce(lam2, lam_pr[:, :, :], AX.X, ALU.add))
            pre(dve.tensor_tensor(tmp8[2], lbt[:, 0:HEADS], lbt[:, HEADS:2 * HEADS], ALU.max))
            dve.wait_ge(v_pre, 5)
            pre(dve.tensor_tensor(tmp8[0], lbt[:, 0:HEADS], tmp8[2], ALU.subtract))
            pre(dve.tensor_tensor(tmp8[1], lbt[:, HEADS:2 * HEADS], tmp8[2], ALU.subtract))
            pre(dve.tensor_copy(ident_bf[:, :], ident[:, :]))
            pre(dve.tensor_scalar(gain_a, lbt[:, 16:17], 0.5, None, ALU.mult))
            pre(dve.tensor_scalar(gain_b, lbt[:, 17:18], 0.5 * (1.0 - LAM_INIT), None, ALU.mult))
            dve.wait_ge(a_pre, 1)
            n = pre(dve.tensor_tensor(neg_lam, lam2[:, 1:2], lam2[:, 0:1], ALU.subtract))
            dve.wait_ge(v_pre, n)
            pre(dve.tensor_scalar(neg_lam, neg_lam, LAM_INIT, None, ALU.subtract))
            dve.wait_ge(a_pre, 3)
            n = pre(dve.tensor_tensor(tmp8[1], tmp8[0], tmp8[1], ALU.add))
            dve.wait_ge(v_pre, n)
            n = pre(dve.reciprocal(tmp8[2], tmp8[1]))
            dve.wait_ge(v_pre, n)
            n = pre(dve.tensor_tensor(tmp8[1], tmp8[0], tmp8[2], ALU.mult))
            dve.wait_ge(v_pre, n)
            pre(dve.tensor_scalar(f_mul, tmp8[1], -0.5, 0.5, ALU.mult, ALU.add))
            n = pre(dve.tensor_scalar(f_neg, tmp8[1], 0.5, -0.5, ALU.mult, ALU.add))
            dve.wait_ge(v_pre, n)
            n = pre(dve.tensor_tensor(f_add, tmp8[1], f_mul, ALU.add))
            dve.wait_ge(x_squared, NT)
            dve.tensor_scalar(ms, ss, 1.0 / D, EPS, ALU.mult, ALU.add).then_inc(x_ms, 1)
            dve.wait_ge(x_rstd, 1)
            for i in range(NT):
                m = P if i < CH else META
                dve.scalar_tensor_tensor(x_in[0:m, i, :], x_in[0:m, i, :], rstd[0:m, i:i + 1], g_in[0:m, :],
                                         ALU.mult, ALU.mult).then_inc(x_normed, 1)
            convert_lo(dve, 0, 0)
            convert_lo(dve, 1, 1)
            for i in range(CH):
                dve.wait_ge(u_ready_hi, i + 1)
                for g in range(2):
                    dst = (a[:, 4 * g:4 * g + 4, META + i * P:META + (i + 1) * P] for a in (uT_lo, uT_hi))
                    ins = dve.tensor_tensor(next(dst), bank(2 * i + g).rearrange("p (k t) -> p k t", k=4),
                                            next(dst).bitcast(F32), ALU.subtract)
                ins.then_inc(u_ready_lo, 1)
            dve.wait_ge(u_ready_hi, NT)
            dve.tensor_tensor(uT_lo[:, :, 0:META], bank(0)[:, 0:KT * META].rearrange("p (k t) -> p k t", k=KT),
                              uT_hi[:, :, 0:META].bitcast(F32), ALU.subtract).then_inc(u_ready_lo, 1)

            with dve.Fori(0, 2) as jj:
                for hh in range(2):
                    for c in range(4):
                        convert_lo(dve, 8 * jj + 4 * hh + c + 2, (c + 2) % 4)
                    dve.wait_ge(w_used, 8 * jj + 4 * hh + 4)
                    for t in ((1, 3), (4, 1))[hh]:
                        b = (t, (5 + t) % 8)[hh]
                        m = P if t < CH else META
                        dve.tensor_copy(v_both[0:m, bass.ds(jj * NT + t, 1), hh * 512:(hh + 1) * 512].rearrange("p a n -> p (a n)"),
                                        bank(b)[0:m, :]).then_inc(vd_taken, 1)
            for n in range(4):
                convert_lo(dve, H0 + n + 2, (n + 2) % 3)

            t_of, at_ = {1: f[:, :]}, 0
            for m in (2, 4, 8, 16, 32, 64, 128):
                n = TOK // m if m <= META else SEQ // m
                t_of[m] = tt[:, at_:at_ + n]
                at_ += n
            OWN = 40

            def head(h, periods):
                count = [0]

                def chain(ins):
                    count[0] += 1
                    ins.then_inc(dve_own, 1)
                    dve.wait_ge(dve_own, OWN * h + count[0])

                def chained():
                    dve.wait_ge(dve_own, OWN * h + count[0])

                def mark(ins):
                    count[0] += 1
                    ins.then_inc(dve_own, 1)

                def conv(p):
                    if p < periods:
                        convert_lo(dve, H0 + 6 * h + 6 + p, p % 3)

                def gate(branch):
                    dve.wait_ge(sec_taken, 6 * h + 5 + branch)
                    dve.scalar_tensor_tensor((gate_a, gate_b)[branch][:, :], th_z[:, :], 1.0, z_g[:, :], ALU.add,
                                             ALU.mult).then_inc(gate_ready, 1)

                def next_level(m):
                    e = LEVELS.index(m) + 1
                    if m > 1:
                        chained()
                    dve.wait_ge(lvl_taken, 8 * h + e)
                    dve.wait_ge(hg_done, hg(h, e))
                    if m < META:
                        kv = kk[:, :].rearrange("p (b two m) -> p b two m", two=2, m=m)
                        tk = t_of[m].rearrange("p (b two) -> p b two", two=2)
                        tq = tk[:, META // (2 * m):, :]
                    else:
                        kv = kk[:, META:].rearrange("p (b two m) -> p b two m", two=2, m=m)
                        t = t_of[m][:, 1:] if m == META else t_of[m]
                        tk = tq = t.rearrange("p (b two) -> p b two", two=2)
                    qv = qq[:, :].rearrange("p (b two m) -> p b two m", two=2, m=m)
                    nk, nq = kv.shape[1], qv.shape[1]
                    dve.tensor_tensor(kv[:, :, 0, :], kv[:, :, 0, :],
                                      tk[:, :, 1:2].to_broadcast([P, nk, m]), ALU.mult)
                    dve.tensor_tensor(qv[:, :, 1, :], qv[:, :, 1, :],
                                      tq[:, :, 0:1].to_broadcast([P, nq, m]), ALU.mult).then_inc(lvl_ready, 1)
                    mark(dve.tensor_tensor(t_of[2 * m], tk[:, :, 0], tk[:, :, 1], ALU.mult))

                def take_level(e):
                    src = bank(LV[e % 2])
                    if e == 0:
                        dve.wait_ge(hg_done, hg(h, 0))
                        dve.tensor_tensor(aa[:, :, :], src.rearrange("p (c t) -> p c t", c=CH),
                                          ident[:, :].rearrange("p (a t) -> p a t", a=1).to_broadcast([P, CH, P]), ALU.mult) \
                            .then_inc(lvl_taken, 1)
                    elif e <= MASKED:
                        m = LEVELS[e - 1]
                        for c in range(CH):
                            dst = aa[:, c, :].rearrange("p (b two m) -> p b two m", two=2, m=m)[:, :, 1, :]
                            ins = dve.copy_predicated(
                                dst, masks[:, e - 1, :].rearrange("p (b m) -> p b m", m=m),
                                src[:, c * 64:(c + 1) * 64].rearrange("p (b m) -> p b m", m=m))
                        ins.then_inc(lvl_taken, 1)
                    else:
                        dve.tensor_copy(aa[0:64, :, 64:128],
                                        src[0:64, 0:CH * 64].rearrange("p (c t) -> p c t", c=CH)) \
                            .then_inc(lvl_taken, 1)

                def norm(branch):
                    dve.wait_ge(o_squared, 2 * h + branch + 1)
                    chain(dve.tensor_reduce(ss[:, 0:CH], sq[:, :, :], AX.X, ALU.add))
                    dve.tensor_scalar(ms[:, 0:CH], ss[:, 0:CH], 1.0 / P, EPS, ALU.mult, ALU.add) \
                        .then_inc(ms_ready, 1)
                    dve.wait_ge(rstd_ready, 2 * h + branch + 1)
                    r = rstd[:, 0:CH].rearrange("p (c a) -> p c a", a=1).to_broadcast([P, CH, P])
                    dve.tensor_tensor(on[:, :, :], bank(B_O).rearrange("p (c d) -> p c d", c=CH), r,
                                      ALU.mult).then_inc(on_ready, 1)

                def gated(branch):
                    dve.wait_ge(*((hg_done, hg(h, 11)) if branch == 0 else (at_done, atn(h, 16))))
                    dve.tensor_tensor((og_a, og_b)[branch][:, bass.ds(h, 1), :].rearrange("p a t -> p (a t)"),
                                      bank((B_OT, B_ATO)[branch]), (gate_a, gate_b)[branch][:, :], ALU.mult) \
                        .then_inc(og_ready, 1)

                def rotate(dst, src, lo):
                    n = src.shape[1]
                    swap = [i + 8 if i < 8 else i - 8 if i < 16 else i for i in range(32)]
                    dve.tensor_tensor(dst, src, rope[:, 0, lo:lo + n], ALU.mult)
                    chain(dve.stream_shuffle(shuf[:, 0:n], src, swap))
                    chain(dve.tensor_tensor(shuf[:, 0:n], shuf[:, 0:n], rope[:, 1, lo:lo + n], ALU.mult))
                    return dve.tensor_tensor(dst, dst, shuf[:, 0:n], ALU.add)

                def row_max(b, comp):
                    n = META + b * P
                    dve.wait_ge(at_done, atn(h, ((0, 1), (3, 5), (7, 9), (11, 13))[b][comp]))
                    chain(dve.tensor_reduce(mx[:, comp:comp + 1], pf[:, SC0 + 512 - n:SC0 + 512 + P], AX.X,
                                            ALU.max))
                    dve.tensor_scalar(nb[:, comp:comp + 1], mx[:, comp:comp + 1], -SCALE, None, ALU.mult) \
                        .then_inc(nb_ready, 1)

                def probs(b):
                    n = META + (b + 1) * P
                    dve.wait_ge(exp_done, 8 * h + 2 * b + 2)
                    chain(dve.reciprocal(rl, lsum))
                    chain(dve.tensor_tensor(rl[:, 1:2], rl[:, 1:2], neg_lam, ALU.mult))
                    chain(dve.tensor_scalar(e1[:, 0:n], e1[:, 0:n], rl[:, 0:1], None, ALU.mult))
                    dve.scalar_tensor_tensor(e1[:, 0:n], e2[:, 0:n], rl[:, 1:2], e1[:, 0:n], ALU.mult, ALU.add) \
                        .then_inc(p_ready, 1)

                dve.wait_ge(sec_taken, 6 * h + 2)
                dve.wait_ge(hg_done, hg(h - 1, 10))
                hcol = bass.ds(h, 1)
                dve.tensor_scalar(kk[:, :], th[:, :], f_neg[:, hcol], f_mul[:, hcol], ALU.mult, ALU.add)
                chain(dve.tensor_scalar(f[:, :], th[:, :], f_mul[:, hcol], f_add[:, hcol], ALU.mult, ALU.add))
                dve.tensor_tensor(qq[:, :], q_raw[:, :], f[:, META:], ALU.mult).then_inc(k_ready, 1)
                dve.wait_ge(k_ready, h + 1)
                conv(0)
                take_level(0)
                next_level(1)
                take_level(1)
                next_level(2)
                take_level(2)
                next_level(4)
                take_level(3)
                gate(0)
                conv(1)
                next_level(8)
                take_level(4)
                next_level(16)
                take_level(5)
                next_level(32)
                take_level(6)
                next_level(64)
                take_level(7)
                gate(1)
                conv(2)
                dve.wait_ge(at_done, atn(h - 1, 13))
                rotate(kT[:, :], ak_raw[:, :], 0)
                dve.wait_ge(hg_done, hg(h, 9))
                chain(dve.tensor_copy(st[:, 0, :], bank(B_G)[:, 0:P]))
                for c in range(CH - 1):
                    ins = dve.scalar_tensor_tensor(st[:, c + 1, :], st[:, c, :], t_of[128][:, c:c + 1],
                                                   bank(B_G)[:, (c + 1) * P:(c + 2) * P], ALU.mult, ALU.add)
                    if c < CH - 2:
                        chain(ins)
                    else:
                        ins.then_inc(st_ready, 1)
                dve.wait_ge(sec_taken, 6 * h + 4)
                rotate(qT[:, :], aq_raw[:, :], META).then_inc(rope_ready, 1)
                norm(0)
                gated(0)
                conv(3)
                row_max(0, 0)
                row_max(0, 1)
                probs(0)
                row_max(1, 0)
                conv(4)
                row_max(1, 1)
                probs(1)
                row_max(2, 0)
                row_max(2, 1)
                probs(2)
                conv(5)
                row_max(3, 0)
                row_max(3, 1)
                probs(3)
                norm(1)
                gated(1)
                assert count[0] <= OWN, count
                while count[0] < OWN:
                    rest = OWN - count[0]
                    count[0] = OWN
                    dve.sem_inc(dve_own, rest)

            with dve.Fori(0, HEADS - 1) as h:
                head(h, 6)
            head(HEADS - 1, 2)

            loc = [0]

            def tchain(ins):
                loc[0] += 1
                ins.then_inc(t_own, 1)
                dve.wait_ge(t_own, loc[0])

            for b, (src, hi, lo) in enumerate(((og_a, oa_hi, oa_lo), (og_b, ob_hi, ob_lo))):
                for k in range(HEADS):
                    dve.wait_ge(og_hi, b * HEADS + k + 1)
                    dve.tensor_tensor(lo[:, k, :], src[:, k, :], hi[:, k, :].bitcast(F32), ALU.subtract) \
                        .then_inc(og_lo, 1)
                    if b == 0 and k in (3, 7):
                        v = k // 4
                        convert_lo(dve, T0 + v + 2, (v + 2) % 4)
            for v in range(T_UNITS + O_UNITS):
                d, j = v // 4, v % 4
                if 2 <= v < T_UNITS + O_UNITS - 2:
                    convert_lo(dve, T0 + v + 2, (v + 2) % 4)
                if j == 1 and 1 <= d <= KT:
                    dve.wait_ge(mhi_ready, d)
                    dve.scalar_tensor_tensor(m_lo[:, d - 1, :], t_m[:, 0, :], 0.5, m_hi[:, d - 1, :].bitcast(F32),
                                             ALU.mult, ALU.subtract).then_inc(mlo_ready, 1)
                if v < T_UNITS and j == 3:
                    if d >= 1:
                        dve.wait_ge(mlo_ready, d)
                    for b in range(2):
                        dve.wait_ge(w_used, T0 + 4 * d + 3 + b)
                        dve.wait_ge(gate_taken, 2 * d + b + 1)
                        dve.scalar_tensor_tensor(t_m[:, b, :], t_gate[:, b, :], 1.0, bank(4 * (d % 2) + 2 + b),
                                                 ALU.add, ALU.mult).then_inc(y_taken, 1)
                    dve.wait_ge(y_taken, 2 * d + 2)
                    dve.tensor_tensor(t_m[:, 0, :], t_m[:, 0, :], t_m[:, 1, :], ALU.add).then_inc(m_sum, 1)
            dve.wait_ge(xres_loaded, 16 * (CH + 1))
            for j in range(2):
                dve.wait_ge(w_used, O0 + 4 * j + 4)
                for t in range(CH):
                    ins = dve.tensor_tensor(y_out[:, t, 512 * j:512 * (j + 1)], bank(4 * j + t),
                                            x_res[:, t, 512 * j:512 * (j + 1)], ALU.add)
                    if j == 1:
                        ins.then_inc(o_taken, 1)
            dve.wait_ge(o_sq, CH)
            dve.tensor_scalar(ms[:, 0:CH], ss[:, 0:CH], 1.0 / D, EPS, ALU.mult, ALU.add).then_inc(o_ms, 1)
            dve.wait_ge(o_rstd, 1)
            for t in range(CH):
                dve.scalar_tensor_tensor(y_out[:, t, :], y_out[:, t, :], rstd[:, t:t + 1], g_fin[:, :], ALU.mult,
                                         ALU.mult).then_inc(y_ready, 1)


_INS = ["x", "meta_tokens", "norm_g", "w_in", "hg_lb_logits", "hg_norm_g", "da_lambda", "da_norm_g",
        "w_branch_a", "w_branch_b", "w_out", "final_g"]


def kernel(**inputs):
    import concourse.bacc as bacc
    from concourse.bass_utils import run_bass_kernel_spmd as run

    nc = bacc.Bacc("TRN2", target_bir_lowering=False, num_devices=1)
    arrays, args = {}, []
    laid = {n: np.ascontiguousarray(inputs[n]) for n in _INS}
    laid.update(constants())
    for name, a in laid.items():
        arrays[f"in_{name}"] = a
        args.append(nc.dram_tensor(f"in_{name}", a.shape, mybir.dt.from_np(a.dtype), kind="ExternalInput").ap())
    args.append(nc.dram_tensor("out_0", (1, SEQ, D), F32, kind="ExternalOutput").ap())
    build(nc, *args)
    r = run(nc, [arrays], core_ids=[0])
    return r.results[0]["out_0"]
```

```python
import numpy as np
import concourse.bass as bass
from concourse import mybir

F32 = mybir.dt.float32
F32R = mybir.dt.float32r
BF16 = mybir.dt.bfloat16
U32 = mybir.dt.uint32
ALU = mybir.AluOpType
ACT = mybir.ActivationFunctionType
AX = mybir.AxisListType

P = 128
D = 1024
SEQ = 512
META = 16
TOK = META + SEQ
KT = D // P
HEADS = D // P
CH = SEQ // P
NT = CH + 1
EPS = 1e-6
LAM_INIT = 0.2
DA_D = 64
SCALE = DA_D ** -0.5
ROPE_DIM = DA_D // 4
ROPE_THETA = 500000.0
NEG = -1e30
LEVELS = [1 << i for i in range(7)]
MASKED = 6
X_ORDER = (0, 1, CH, 2, 3)
HQ, HF, HI, HZ, AQ, AK, AV, AZ, GA, GB = (i * D for i in range(10))

UNIT = 1024
SLOTS = 4
SECTIONS = 8
COLS = (HF, HQ, AK, AQ, HI, HZ, AV, AZ)
AHEAD = 4
T0 = SECTIONS * HEADS
T_UNITS = 4 * KT
O0 = T0 + T_UNITS
ALL_UNITS = O0 + 8

HG_STEPS = ["diag", "l1", "l2", "l4", "l8", "l16", "l32", "l64", "keys", "values", "sums", "out", "turn"]
AT_STEPS = ["s0", "s1", "values", "t0", "s2", "a0", "t1", "a1", "t2", "s3", "a2", "t3", "a3", "turn"]
HG, AT = len(HG_STEPS), len(AT_STEPS)
HG_AT = dict(zip(HG_STEPS, (3, 6, 9, 12, 15, 18, 21, 24, 27, 29, 32, 35, 40)))
AT_AT = dict(zip(AT_STEPS, (20, 25, 28, 30, 31, 33, 36, 38, 42, 44, 46, 51, 54, 60)))


def constants():
    ident = np.eye(P, dtype=np.float32)
    q, k = np.arange(P)[:, None], np.arange(P)[None, :]
    bias = np.where(k <= q, np.float32(0), np.float32(NEG)).astype(np.float32)
    masks = np.zeros((P, MASKED, P // 2), np.uint32)
    s = np.arange(P)[:, None]
    j = np.arange(P // 2)[None, :]
    for i, m in enumerate(LEVELS[:MASKED]):
        t = (j // m) * 2 * m + m + j % m
        masks[:, i, :] = (s // (2 * m) == t // (2 * m)) & (s % (2 * m) < m)
    half = ROPE_DIM // 2
    inv = np.float32(ROPE_THETA) ** (-np.arange(half, dtype=np.float32) * np.float32(2.0) / np.float32(ROPE_DIM))
    ang = np.arange(TOK, dtype=np.float32)[None, :] * inv.astype(np.float32)[:, None]
    cos, sin = np.cos(ang), np.sin(ang)
    rope = np.zeros((P, 2, TOK), np.float32)
    rope[:, 0, :] = 1.0
    for c in (0, DA_D):
        rope[c:c + half, 0], rope[c + half:c + ROPE_DIM, 0] = cos, cos
        rope[c:c + half, 1], rope[c + half:c + ROPE_DIM, 1] = -sin, sin
    return {"c_ident": ident, "c_bias": bias, "c_masks": masks, "c_rope": rope}


def build(nc, x, meta_tokens, norm_g, w_in, lb_logits, hg_norm_g, da_lambda, da_norm_g,
          w_branch_a, w_branch_b, w_out, final_g, c_ident, c_bias, c_masks, c_rope, out):
    x = x.rearrange("b s d -> (b s) d")
    out = out.rearrange("b s d -> (b s) d")
    w_in = w_in.rearrange("l (k p) n -> p (l k) n", p=P)
    w_branch_a = w_branch_a.rearrange("l (k p) n -> p (l k) n", p=P)
    w_branch_b = w_branch_b.rearrange("l (k p) n -> p (l k) n", p=P)
    w_out = w_out.rearrange("l (k p) n -> p (l k) n", p=P)

    def at(name, shape, dt, offset):
        size = int(np.prod(shape[1:])) * (2 if dt == BF16 else 4)
        return nc.alloc_sbuf_tensor_at(name, shape, dt, offset=offset), offset + (size + 31) // 32 * 32

    base = 16512
    uT_hi, o = at("uT_hi", [P, KT, TOK], F32R, base)
    uT_lo, o = at("uT_lo", [P, KT, TOK], F32R, o)
    w_raw, o = at("w_raw", [P, SLOTS, UNIT], F32, o)
    w_hi, o = at("w_hi", [P, SLOTS, UNIT], F32R, o)
    w_lo, o = at("w_lo", [P, SLOTS, UNIT], F32R, o)
    region_o = o
    x_in, o2 = at("x_in", [P, NT, D], F32, region_o)
    g_in, o2 = at("g_in", [P, D], F32, o2)
    x_sq, o2 = at("x_sq", [P, D], F32, o2)
    oa_hi, o = at("oa_hi", [P, KT, SEQ], F32R, region_o)
    oa_lo, o = at("oa_lo", [P, KT, SEQ], F32R, o)
    ob_hi, o = at("ob_hi", [P, KT, SEQ], F32R, o)
    ob_lo, o = at("ob_lo", [P, KT, SEQ], F32R, o)
    y_out, o3 = at("y_out", [P, CH, D], F32, region_o)
    y_sq, o3 = at("y_sq", [P, SEQ], F32, o3)
    ident, o = at("ident", [P, P], F32, o)
    ident_bf, o = at("ident_bf", [P, P], BF16, o)
    bias_bf, o = at("bias_bf", [P, P], BF16, o)
    masks, o = at("masks", [P, MASKED, P // 2], U32, o)
    rope, o = at("rope", [P, 2, TOK], F32, o)
    small, o = at("small", [P, 128], F32, o)
    region_w = o
    f, o = at("f", [P, TOK], F32, o)
    tt, o = at("tt", [P, TOK], F32, o)
    q_raw, o = at("q_raw", [P, SEQ], F32, o)
    aa, o = at("aa", [P, CH, P], F32, o)
    tg, _ = at("tg", [P, 4, SEQ], F32, region_w)
    region_m = o
    kk, o = at("kk", [P, TOK], F32, o)
    qq, o = at("qq", [P, SEQ], F32, o)
    k_tok, o = at("k_tok", [P, CH, P], F32, o)
    st, o = at("st", [P, CH, P], F32, o)
    sq, o = at("sq", [P, CH, P], F32, o)
    on, o = at("on", [P, CH, P], F32, o)
    og, o = at("og", [P, SEQ], F32, o)
    th_z, o = at("th_z", [P, SEQ], F32, o)
    z_g, o = at("z_g", [P, SEQ], F32, o)
    gate_a, o = at("gate_a", [P, SEQ], F32, o)
    gate_b, o = at("gate_b", [P, SEQ], F32, o)
    kT, o = at("kT", [P, TOK], F32, o)
    qT, o = at("qT", [P, SEQ], F32, o)
    e1, o = at("e1", [P, 2, TOK], F32, o)
    e2, o = at("e2", [P, 2, TOK], F32, o)
    shuf = e2[:, 1, :]
    pT, o = at("pT", [P, NT, P], F32, o)
    vT_a, o = at("vT_a", [P, TOK], F32, o)
    vT_b, o = at("vT_b", [P, TOK], F32, o)
    v_a, o = at("v_a", [P, NT, P], F32, o)
    v_b, o = at("v_b", [P, NT, P], F32, o)
    lam_in, _ = at("lam_in", [P, 4, DA_D], F32, region_w)
    rows_in, _ = at("rows_in", [2 * HEADS + 2, P], F32, region_w + 4096)
    bias_in, _ = at("bias_in", [P, P], F32, region_w + 8192)
    lam_pr, _ = at("lam_pr", [P, 2, DA_D], F32, region_w + 12288)
    m_hi, o2 = at("m_hi", [P, KT, SEQ], F32R, region_m)
    m_lo, o2 = at("m_lo", [P, KT, SEQ], F32R, o2)
    t_gate, o2 = at("t_gate", [P, 2, SEQ], F32, o2)
    t_m, o2 = at("t_m", [P, 2, SEQ], F32, o2)
    x_res, o3 = at("x_res", [P, CH, D], F32, base)
    g_fin, o3 = at("g_fin", [P, D], F32, o3)

    taken = [0]

    def cols(n):
        taken[0] += n
        return small[:, taken[0] - n:taken[0]]

    lbt = cols(2 * HEADS + 2)
    f_mul, f_neg, f_add, e_0, e_1, e_m = (cols(HEADS) for _ in range(6))
    gain_a, gain_b, neg_lam, lam2, warm = cols(1), cols(1), cols(1), cols(2), cols(NT)
    ss, ms, rstd, half_neg, ss2 = (cols(NT) for _ in range(5))
    mx, nb, lsum, rl, mx2, lsum2 = (cols(2) for _ in range(6))

    ps = nc.alloc_psum_tensor("ps", [P, 8, 512], F32)

    def bank(i):
        return ps[:, i, :]

    B_HG, B_S, B_T, B_A = 3, 4, 6, 7
    PAIR = ps[:, 0:2, 0:TOK // 2]

    sem = nc.alloc_semaphore
    ident_in, norm_in, meta_in, rows_ready, tables_in = (sem(n) for n in (
        "ident_in", "norm_in", "meta_in", "rows_ready", "tables_in"))
    x_loaded = [sem(f"x_loaded{i}") for i in range(CH)]
    xres_loaded, stored = sem("xres_loaded"), sem("stored")
    w_loaded = [sem(f"w_loaded{i}") for i in range(SLOTS)]
    slot_free = sem("slot_free")
    hi_ready, lo_ready, w_used = sem("hi_ready"), sem("lo_ready"), sem("w_used")
    v_pre, a_pre, g_pre, pe_pre = sem("v_pre"), sem("a_pre"), sem("g_pre"), sem("pe_pre")
    u_ready_hi, u_ready_lo = sem("u_ready_hi"), sem("u_ready_lo")
    x_squared, x_ms, x_rstd, x_normed, x_turned = (sem(n) for n in (
        "x_squared", "x_ms", "x_rstd", "x_normed", "x_turned"))
    sec_taken = sem("sec_taken")
    dve_own = sem("dve_own")
    k_ready, lvl_ready, lvl_taken = sem("k_ready"), sem("lvl_ready"), sem("lvl_taken")
    hg_done, at_done = sem("hg_done"), sem("at_done")
    ktok_ready, va_ready, vb_ready, st_ready = sem("ktok_ready"), sem("va_ready"), sem("vb_ready"), sem("st_ready")
    o_squared, ms_ready, rstd_ready, on_ready, og_ready, oghi_ready, oglo_ready = (sem(n) for n in (
        "o_squared", "ms_ready", "rstd_ready", "on_ready", "og_ready", "oghi_ready", "oglo_ready"))
    rope_ready, gate_ready = sem("rope_ready"), sem("gate_ready")
    meta_scored = sem("meta_scored")
    nb_ready, exp_done, p_ready, pT_ready = sem("nb_ready"), sem("exp_done"), sem("p_ready"), sem("pT_ready")
    gate_taken, y_taken, m_sum, mhi_ready, mlo_ready = (sem(n) for n in (
        "gate_taken", "y_taken", "m_sum", "mhi_ready", "mlo_ready"))
    o_done, o_taken, o_sq, o_own, o_ms, o_rstd, y_ready = (sem(n) for n in (
        "o_done", "o_taken", "o_sq", "o_own", "o_ms", "o_rstd", "y_ready"))

    def convert_hi(act, u, slot, loads):
        act.wait_ge(w_loaded[slot], 16 * loads)
        if not isinstance(u, int) or u >= SLOTS:
            act.wait_ge(w_used, u - SLOTS + 1)
        act.activation(w_hi[:, slot, :], w_raw[:, slot, :], ACT.Copy).then_inc(hi_ready, 1)

    def convert_lo(eng, u, slot):
        eng.wait_ge(hi_ready, u + 1)
        eng.tensor_tensor(w_lo[:, slot, :], w_raw[:, slot, :], w_hi[:, slot, :].bitcast(F32),
                          ALU.subtract).then_inc(lo_ready, 1)

    def hg(h, step):
        return HG * (h + 1) + HG_STEPS.index(step) + 1

    def atn(h, step):
        return AT * (h + 1) + AT_STEPS.index(step) + 1

    def n_keys(b):
        return META + (b + 1) * P

    block = nc.Block()
    with block:
        @block.sync
        def _(sp):
            def load(u, slot, src):
                if not isinstance(u, int):
                    sp.wait_ge(lo_ready, u - SLOTS + 1)
                    sp.sem_inc(slot_free, 1)
                elif u >= SLOTS:
                    sp.wait_ge(lo_ready, u - SLOTS + 1)
                sp.dma_start(w_raw[:, slot, :].rearrange("p (k n) -> p k n", k=src.shape[1]), src) \
                    .then_inc(w_loaded[slot], 16)

            def section(h, s, u, slot):
                load(u, slot, w_in[:, :, bass.ds(h * P + COLS[s], P)])

            for i in range(CH):
                sp.dma_start(x_in[:, i, :], x[i * P:(i + 1) * P, :]).then_inc(x_loaded[i], 16)
                if i == 1:
                    section(0, 0, 0, 0)
            section(0, 1, 1, 1)
            sp.dma_start(rows_in[0:2 * HEADS, :], lb_logits.rearrange("r (h p) -> (r h) p", p=P)) \
                .then_inc(rows_ready, 16)
            sp.dma_start(rows_in[2 * HEADS:2 * HEADS + 1, :], hg_norm_g).then_inc(rows_ready, 16)
            sp.dma_start(rows_in[2 * HEADS + 1:2 * HEADS + 2, :], da_norm_g).then_inc(rows_ready, 16)
            section(0, 2, 2, 2)
            sp.dma_start(lam_in[:, :, :].rearrange("p r d -> p (r d)"),
                         da_lambda.rearrange("l r d -> l (r d)").to_broadcast([P, 4 * DA_D])) \
                .then_inc(tables_in, 16)
            sp.dma_start(bias_in[:, :], c_bias).then_inc(tables_in, 16)
            section(0, 3, 3, 3)
            sp.dma_start(masks[:, :, :], c_masks).then_inc(tables_in, 16)
            sp.dma_start(rope[:, :, :], c_rope).then_inc(tables_in, 16)
            with sp.Fori(0, HEADS - 1) as h:
                for p in range(SECTIONS):
                    section(h if p < 4 else h + 1, (p + 4) % 8, SECTIONS * h + AHEAD + p, p % 4)
            for p in range(SECTIONS - AHEAD):
                section(HEADS - 1, AHEAD + p, T0 - 4 + p, p)
            for d in range(2):
                for j, col in enumerate((GA, GB)):
                    load(T0 + 2 * d + j, 2 * d + j, w_in[:, :, col + d * P:col + (d + 1) * P])
            for d in range(2):
                for j, w in enumerate((w_branch_a, w_branch_b)):
                    load(T0 + 4 + 2 * d + j, 2 * d + j, w[:, :, d * P:(d + 1) * P])
            with sp.Fori(0, KT // 2 - 1) as i:
                for dd in range(2):
                    u = T0 + 8 + 8 * i + 4 * dd
                    at_d = i * (2 * P) + (2 + dd) * P
                    load(u, 0, w_in[:, :, bass.ds(at_d + GA, P)])
                    load(u + 1, 1, w_in[:, :, bass.ds(at_d + GB, P)])
                    load(u + 2, 2, w_branch_a[:, :, bass.ds(at_d, P)])
                    load(u + 3, 3, w_branch_b[:, :, bass.ds(at_d, P)])
            for c in range(4):
                load(O0 + c, c, w_out[:, 2 * c:2 * c + 2, 0:512])
            sp.wait_ge(w_used, O0 - 2)
            for i in range(CH):
                sp.dma_start(x_res[:, i, :], x[i * P:(i + 1) * P, :]).then_inc(xres_loaded, 16)
            sp.dma_start(g_fin[:, :], final_g.rearrange("(a n) -> a n", a=1).to_broadcast([P, D])) \
                .then_inc(xres_loaded, 16)
            for c in range(4):
                load(O0 + 4 + c, c, w_out[:, 2 * c:2 * c + 2, 512:1024])
            for i in range(CH):
                sp.wait_ge(y_ready, i + 1)
                sp.dma_start(out[i * P:(i + 1) * P, :], y_out[:, i, :]).then_inc(stored, 16)
            sp.wait_ge(stored, 16 * CH)

        @block.gpsimd
        def _(pool):
            pool.memset(half_neg, -0.5).then_inc(g_pre, 1)
            pool.wait_ge(g_pre, 1)
            for n, i in enumerate(X_ORDER):
                m = P if i < CH else META
                pool.wait_ge(x_ms, n + 1)
                pool.tensor_tensor(rstd[0:m, i:i + 1], ms[0:m, i:i + 1], half_neg[0:m, 0:1], ALU.pow) \
                    .then_inc(x_rstd, 1)
            with pool.Fori(0, 2 * HEADS) as b:
                pool.wait_ge(ms_ready, b + 1)
                pool.tensor_tensor(rstd[:, 0:CH], ms[:, 0:CH], half_neg[:, 0:CH], ALU.pow).then_inc(rstd_ready, 1)
            for t in range(CH):
                pool.wait_ge(o_ms, t + 1)
                pool.tensor_tensor(rstd[:, t:t + 1], ms[:, t:t + 1], half_neg[:, 0:1], ALU.pow).then_inc(o_rstd, 1)

        @block.tensor
        def _(pe):
            def three(dst, w, rhs, start, stop):
                pe.matmul(dst, w[0], rhs[0], start=start, stop=False, skip_group_check=True)
                pe.matmul(dst, w[0], rhs[1], start=False, stop=False, skip_group_check=True)
                return pe.matmul(dst, w[1], rhs[0], start=False, stop=stop, skip_group_check=True)

            def turn_x(n):
                i = X_ORDER[n]
                pe.wait_ge(x_normed, n + 1)
                if i == CH:
                    pe.wait_ge(v_pre, 1)
                elif n > 2:
                    pe.wait_ge(u_ready_lo, n - 2)
                for k in range(KT):
                    if i == CH:
                        t = pe.transpose(bank(3)[:, k * META:(k + 1) * META], x_in[0:META, CH, k * P:(k + 1) * P],
                                         ident[0:META, 0:META])
                    else:
                        t = pe.transpose(bank(4 + 2 * (i % 2) + k // 4)[:, (k % 4) * P:(k % 4 + 1) * P],
                                         x_in[:, i, k * P:(k + 1) * P], ident[:, :])
                t.then_inc(x_turned, 1)

            def groups(n, s, slot, ks):
                if ks[0] == 0:
                    pe.wait_ge(lo_ready, n + 1)
                    if not isinstance(n, int) or n >= 2:
                        pe.wait_ge(sec_taken, n - 1)
                for k in ks:
                    w = tuple(a[:, slot, k * P:(k + 1) * P] for a in (w_hi, w_lo))
                    if s % 2 == 0:
                        for b in range(2):
                            rhs = tuple(a[:, k, b * (TOK // 2):(b + 1) * (TOK // 2)] for a in (uT_hi, uT_lo))
                            last = three(PAIR[:, b, :], w, rhs, k == 0, k == KT - 1)
                    else:
                        rhs = tuple(a[:, k, META:TOK] for a in (uT_hi, uT_lo))
                        last = three(bank(2), w, rhs, k == 0, k == KT - 1)
                    if k == KT - 1:
                        last.then_inc(w_used, 1)

            def merge_gate(i, ks):
                n = T0 + i
                if ks[0] == 0:
                    pe.wait_ge(lo_ready, n + 1)
                    pe.wait_ge(sec_taken, n - 1)
                for k in ks:
                    w = tuple(a[:, i, k * P:(k + 1) * P] for a in (w_hi, w_lo))
                    rhs = tuple(a[:, k, META:TOK] for a in (uT_hi, uT_lo))
                    last = three(bank(0 if i % 2 == 0 else 2), w, rhs, k == 0, k == KT - 1)
                if ks[-1] == KT - 1:
                    last.then_inc(w_used, 1)

            def half_section(s, half):
                n = (TOK if s == 0 else SEQ) // 2
                dst = PAIR[:, half, :] if s == 0 else bank(2)[:, half * n:(half + 1) * n]
                at_t = half * n + TOK - 2 * n
                pe.wait_ge(lo_ready, s + 1)
                pe.wait_ge(u_ready_lo, (3, NT)[half])
                for k in range(KT):
                    last = three(dst, tuple(a[:, s, k * P:(k + 1) * P] for a in (w_hi, w_lo)),
                                 tuple(a[:, k, at_t:at_t + n] for a in (uT_hi, uT_lo)), k == 0, k == KT - 1)
                if half == 1:
                    last.then_inc(w_used, 1)

            pe.wait_ge(ident_in, 16)
            turn_x(0)
            turn_x(1)
            pe.wait_ge(rows_ready, 48)
            pe.transpose(bank(3)[:, 256:256 + 2 * HEADS + 2], rows_in[:, :], ident[0:2 * HEADS + 2, 0:2 * HEADS + 2]) \
                .then_inc(pe_pre, 1)
            turn_x(2)
            turn_x(3)
            half_section(0, 0)
            turn_x(4)
            half_section(1, 0)
            half_section(0, 1)
            half_section(1, 1)
            for s in range(2, AHEAD):
                groups(s, s, s, range(KT))

            def level(h, e):
                dst = bank(B_HG)
                if e == 0:
                    pe.wait_ge(k_ready, h + 1)
                    pe.wait_ge(og_ready, 2 * h + 1)
                else:
                    if e >= 2:
                        pe.wait_ge(lvl_ready, 7 * h + e - 1)
                    pe.wait_ge(lvl_taken, 8 * h + e)
                if e == 7:
                    pe.wait_ge(sec_taken, SECTIONS * h + 5)
                    pe.transpose(dst[0:META, 256:256 + P], vT_a[:, 0:META], ident[:, :])
                for c in range(CH):
                    kc = kk[:, META + c * P:META + (c + 1) * P]
                    qc = qq[:, c * P:(c + 1) * P]
                    if e == 0:
                        mm = pe.matmul(dst[:, c * P:(c + 1) * P], kc, q_raw[:, c * P:(c + 1) * P],
                                       start=True, stop=True)
                    elif e <= MASKED:
                        m = LEVELS[e - 1]
                        second = qc.rearrange("p (b two m) -> p b two m", two=2, m=m)[:, :, 1, :]
                        mm = pe.matmul(dst[:, c * 64:(c + 1) * 64].rearrange("p (b m) -> p b m", m=m),
                                       kc, second, start=True, stop=True)
                    else:
                        mm = pe.matmul(dst[0:64, c * 64:(c + 1) * 64], kc[:, 0:64], qc[:, 64:128],
                                       start=True, stop=True)
                mm.then_inc(hg_done, 1)

            def keys_token_major(h):
                pe.wait_ge(lvl_ready, 7 * h + 7)
                pe.wait_ge(lvl_taken, 8 * h + 8)
                for c in range(CH - 1):
                    pe.transpose(bank(B_HG)[:, c * P:(c + 1) * P],
                                 kk[:, META + c * P:META + (c + 1) * P], ident[:, :])
                pe.transpose(bank(B_HG)[0:META, (CH - 1) * P:], kk[:, 0:META], ident[:, :]).then_inc(hg_done, 1)

            def values_token_major(vT, b, done):
                for c in range(CH):
                    mm = pe.transpose(bank(b)[:, c * P:(c + 1) * P],
                                      vT[:, META + c * P:META + (c + 1) * P], ident[:, :])
                mm.then_inc(done, 1)

            def state_sums(h):
                pe.wait_ge(va_ready, h + 1)
                g = bank(B_HG)
                for c in range(CH - 1):
                    pe.matmul(g[:, (c + 1) * P:(c + 2) * P], k_tok[:, c, :], v_a[:, c, :], start=True, stop=True)
                pe.matmul(g[:, 0:P], k_tok[0:META, CH - 1, :], v_a[0:META, CH, :], start=True, stop=True) \
                    .then_inc(hg_done, 1)

            def outputs(h):
                pe.wait_ge(st_ready, h + 1)
                for c in range(CH):
                    dst = bank(B_HG)[:, c * P:(c + 1) * P]
                    pe.matmul(dst, aa[:, c, :], v_a[:, c, :], start=True, stop=False)
                    mm = pe.matmul(dst, qq[:, c * P:(c + 1) * P], st[:, c, :], start=False, stop=True)
                mm.then_inc(hg_done, 1)

            def turn(h, branch, b, done):
                pe.wait_ge(on_ready, 2 * h + 1 + branch)
                for c in range(CH):
                    mm = pe.transpose(bank(b)[:, c * P:(c + 1) * P], on[:, c, :], ident[:, :])
                mm.then_inc(done, 1)

            def scores(h, b):
                if b == 0:
                    pe.wait_ge(rope_ready, h + 1)
                else:
                    pe.wait_ge(exp_done, 8 * h + 2 * b)
                if b == CH - 1:
                    pe.wait_ge(pT_ready, 4 * h + b)
                n = n_keys(b)
                at_k = 0 if b < CH - 1 else META
                w = n - P - at_k
                half = [slice(comp * DA_D, (comp + 1) * DA_D) for comp in range(2)]
                q = [qT[r, b * P:(b + 1) * P] for r in half]

                def meta(comp):
                    return pe.matmul(bank(B_T)[:, comp * META:(comp + 1) * META], q[comp],
                                     kT[half[comp], 0:META], start=True, stop=True)

                if b == CH - 1:
                    meta(0).then_inc(meta_scored, 1)
                for comp in range(2):
                    pe.matmul(bank(B_S + comp)[:, 0:w], q[comp], kT[half[comp], at_k:n - P], start=True, stop=True)
                for comp in range(2):
                    pe.matmul(bank(B_S + comp)[:, w:w + P], q[comp], kT[half[comp], n - P:n],
                              start=True, stop=False)
                if b == CH - 1:
                    pe.wait_ge(meta_scored, h + 1)
                    meta(1)
                for comp in range(2):
                    mm = pe.matmul(bank(B_S + comp)[:, w:w + P], ident_bf[:, :], bias_bf[:, :],
                                   start=False, stop=True)
                mm.then_inc(at_done, 1)

            def turn_probs(h, b):
                pe.wait_ge(p_ready, 4 * h + b + 1)
                p = e1[:, b % 2, :]
                if b == 0:
                    pe.wait_ge(vb_ready, h + 1)
                    pe.transpose(bank(B_T)[0:META, 256:256 + P], vT_b[:, 0:META], ident[:, :])
                else:
                    pe.wait_ge(pT_ready, 4 * h + b)
                for j in range(b + 1):
                    pe.transpose(bank(B_T)[:, j * P:(j + 1) * P], p[:, META + j * P:META + (j + 1) * P],
                                 ident[:, :])
                dst = bank(B_T if b < CH - 1 else B_A)[0:META, 3 * P:]
                pe.transpose(dst, p[:, 0:META], ident[:, :]).then_inc(at_done, 1)

            def attend(h, b):
                pe.wait_ge(pT_ready, 4 * h + b + 1)
                dst = bank(B_A)[:, b * P:(b + 1) * P]
                for j in range(b + 1):
                    pe.matmul(dst, pT[:, j, :], v_b[:, j, :], start=(j == 0), stop=False)
                pe.matmul(dst, pT[0:META, CH, :], v_b[0:META, CH, :], start=False, stop=True) \
                    .then_inc(at_done, 1)

            def head(h, last):
                for t in range(SECTIONS * KT):
                    p, g = t // KT, t % KT
                    if p < SECTIONS - AHEAD or not last:
                        groups(SECTIONS * h + AHEAD + p, (p + AHEAD) % SECTIONS, p % SLOTS, [g])
                    else:
                        merge_gate(p - 4, [g])
                    for e in range(8):
                        if t == HG_AT[HG_STEPS[e]]:
                            level(h, e)
                    for b in range(2):
                        if t == AT_AT[f"s{b}"]:
                            scores(h, b)
                    if t == HG_AT["keys"]:
                        keys_token_major(h)
                    if t == AT_AT["values"]:
                        pe.wait_ge(sec_taken, SECTIONS * h + 7)
                        pe.wait_ge(og_ready, 2 * h + 2)
                        values_token_major(vT_b, B_T, at_done)
                    if t == HG_AT["values"]:
                        pe.wait_ge(ktok_ready, h + 1)
                        values_token_major(vT_a, B_HG, hg_done)
                    if t == HG_AT["sums"]:
                        state_sums(h)
                    if t == HG_AT["out"]:
                        outputs(h)
                    if t == HG_AT["turn"]:
                        turn(h, 0, B_HG, hg_done)
                    for b in range(CH):
                        if t == AT_AT[f"t{b}"]:
                            turn_probs(h, b)
                        if b >= 2 and t == AT_AT[f"s{b}"]:
                            scores(h, b)
                        if t == AT_AT[f"a{b}"]:
                            attend(h, b)
                    if t == AT_AT["turn"]:
                        turn(h, 1, B_T, at_done)

            with pe.Fori(0, HEADS - 1) as h:
                head(h, False)
            head(HEADS - 1, True)

            def product(u, slot, rhs, dst):
                pe.wait_ge(lo_ready, u + 1)
                for k in range(KT):
                    w = tuple(a[:, slot, k * P:(k + 1) * P] for a in (w_hi, w_lo))
                    last = three(dst, w, tuple(a[:, k, :] for a in rhs), k == 0, k == KT - 1)
                last.then_inc(w_used, 1)

            u_x = tuple(a[:, :, META:TOK] for a in (uT_hi, uT_lo))
            branches = (oa_hi, oa_lo), (ob_hi, ob_lo)
            pe.wait_ge(sec_taken, T0 + 4)
            pe.wait_ge(oglo_ready, 2 * HEADS)
            for d in range(2):
                for j in range(2):
                    product(T0 + 4 + 2 * d + j, 2 * d + j, branches[j], bank(4 * d + 2 + j))
            with pe.Fori(0, KT // 2 - 1) as i:
                for dd in range(2):
                    u = T0 + 8 + 8 * i + 4 * dd
                    for j in range(2):
                        pe.wait_ge(gate_taken, 4 * i + 2 * dd + j + 1)
                        product(u + j, j, u_x, bank(4 * dd + j))
                    for j in range(2):
                        pe.wait_ge(y_taken, 4 * i + 2 * dd + j + 1)
                        product(u + 2 + j, 2 + j, branches[j], bank(4 * dd + 2 + j))
            pe.wait_ge(y_taken, 2 * KT - 2)
            for j in range(2):
                for c in range(4):
                    pe.wait_ge(lo_ready, O0 + 4 * j + c + 1)
                    if j == 1 and c == 0:
                        pe.wait_ge(y_taken, 2 * KT)
                    if j == 0:
                        pe.wait_ge(mlo_ready, 2 * c + 2)
                    for t in range(CH):
                        for k in range(2):
                            mt = tuple(a[:, 2 * c + k, t * P:(t + 1) * P] for a in (m_hi, m_lo))
                            ws = tuple(a[:, c, 512 * k:512 * (k + 1)] for a in (w_hi, w_lo))
                            last = three(bank(4 * j + t), mt, ws, c == 0 and k == 0, c == 3 and k == 1)
                        if c == 3 and t < CH - 1:
                            last.then_inc(o_done, 1)
                    last.then_inc(w_used, 1)

        @block.scalar
        def _(act):
            act.dma_start(ident[:, :], c_ident).then_inc(ident_in, 16)
            act.dma_start(g_in[:, :], norm_g.to_broadcast([P, D])).then_inc(norm_in, 16)
            act.dma_start(x_in[0:META, CH, :], meta_tokens).then_inc(meta_in, 16)
            act.wait_ge(g_pre, 1)
            act.activation(warm, half_neg, ACT.Square)
            act.sem_inc(og_ready, 2)
            act.sem_inc(hg_done, HG)
            act.sem_inc(at_done, AT)
            act.sem_inc(gate_ready, 2)
            act.sem_inc(oghi_ready, 2)
            act.sem_inc(gate_taken, 4)

            def square_x(n):
                i = X_ORDER[n]
                m = P if i < CH else META
                act.wait_ge(*((x_loaded[i], 16) if i < CH else (meta_in, 16)))
                if n > 0:
                    act.wait_ge(x_squared, n)
                act.activation(x_sq[0:m, :], x_in[0:m, i, :], ACT.Square, accum_out=ss[0:m, i:i + 1]) \
                    .then_inc(x_squared, 1)

            def turned_x(n):
                i = X_ORDER[n]
                act.wait_ge(x_turned, n + 1)
                if i == CH:
                    act.activation(uT_hi[:, :, 0:META], bank(3)[:, 0:KT * META].rearrange("p (k t) -> p k t", k=KT),
                                   ACT.Copy).then_inc(u_ready_hi, 1)
                    return
                for g in range(2):
                    ins = act.activation(uT_hi[:, 4 * g:4 * g + 4, META + i * P:META + (i + 1) * P],
                                         bank(4 + 2 * (i % 2) + g).rearrange("p (k t) -> p k t", k=4), ACT.Copy)
                ins.then_inc(u_ready_hi, 1)

            square_x(0)
            square_x(1)
            square_x(2)
            turned_x(0)
            square_x(3)
            convert_hi(act, 0, 0, 1)
            turned_x(1)
            square_x(4)
            turned_x(2)
            turned_x(3)
            convert_hi(act, 1, 1, 1)
            turned_x(4)
            convert_hi(act, 2, 2, 1)
            act.wait_ge(v_pre, 4)
            act.activation(lam2, lam2, ACT.Exp).then_inc(a_pre, 1)
            act.wait_ge(v_pre, 7)
            act.activation(e_0, e_0, ACT.Exp).then_inc(a_pre, 1)
            act.activation(e_1, e_1, ACT.Exp).then_inc(a_pre, 1)

            def take(h, s):
                act.wait_ge(w_used, SECTIONS * h + s + 1)
                first = isinstance(h, int) and h == 0
                pair = lambda t: t.rearrange("p (b t) -> p b t", b=2)
                if s == 0:
                    act.wait_ge(hg_done, hg(h - 1, "keys"))
                    act.activation(pair(kk[:, :]), PAIR, ACT.Tanh, scale=0.5).then_inc(sec_taken, 1)
                elif s == 1:
                    act.wait_ge(hg_done, hg(h - 1, "diag"))
                    act.activation(q_raw[:, :], bank(2), ACT.Copy).then_inc(sec_taken, 1)
                elif s == 2:
                    act.wait_ge(at_done, atn(h - 1, "s3"))
                    act.activation(pair(kT[:, :]), PAIR, ACT.Copy).then_inc(sec_taken, 1)
                elif s == 3:
                    act.wait_ge(at_done, atn(h - 1, "s3"))
                    act.activation(qT[:, :], bank(2), ACT.Copy).then_inc(sec_taken, 1)
                elif s == 4:
                    act.wait_ge(hg_done, hg(h - 1, "values"))
                    act.activation(pair(vT_a[:, :]), PAIR, ACT.Copy).then_inc(sec_taken, 1)
                elif s == 6:
                    act.wait_ge(at_done, atn(h - 1, "t0"))
                    act.activation(pair(vT_b[:, :]), PAIR, ACT.Copy).then_inc(sec_taken, 1)
                else:
                    act.wait_ge(gate_ready, 2 * h + (2 if s == 5 else 3))
                    act.activation(th_z[:, :], bank(2), ACT.Tanh, scale=0.5)
                    act.activation(z_g[:, :], bank(2), ACT.Copy, scale=(gain_a if s == 5 else gain_b)) \
                        .then_inc(sec_taken, 1)

            for n in range(AHEAD):
                convert_hi(act, n + 3, (n + 3) % SLOTS, (n + 3) // SLOTS + 1)
                if n > 0:
                    take(0, n - 1)

            def square(h, branch, b, done, step):
                act.wait_ge(done, step)
                act.activation(sq[:, :, :].rearrange("p c d -> p (c d)"), bank(b), ACT.Square) \
                    .then_inc(o_squared, 1)

            def exps(h, b):
                act.wait_ge(nb_ready, 4 * h + b + 1)
                act.wait_ge(at_done, atn(h - 1, f"t{b + 2}") if b < 2 else atn(h, f"t{b - 2}"))
                n = n_keys(b)
                for comp in range(2):
                    e = (e1, e2)[comp][:, b % 2, :]
                    if b < CH - 1:
                        ins = act.activation(e[:, 0:n], bank(B_S + comp)[:, 0:n], ACT.Exp, bias=nb[:, comp:comp + 1],
                                             scale=SCALE, accum_out=lsum[:, comp:comp + 1])
                    else:
                        act.activation(e[:, 0:META], bank(B_T)[:, comp * META:(comp + 1) * META], ACT.Exp,
                                       bias=nb[:, comp:comp + 1], scale=SCALE, accum_out=lsum2[:, comp:comp + 1])
                        ins = act.activation(e[:, META:n], bank(B_S + comp), ACT.Exp, bias=nb[:, comp:comp + 1],
                                             scale=SCALE, accum_out=lsum[:, comp:comp + 1])
                    ins.then_inc(exp_done, 1)

            def probs_out(h, b):
                act.wait_ge(at_done, atn(h, f"t{b}"))
                if b == 0:
                    act.activation(v_b[0:META, CH, :], bank(B_T)[0:META, 256:256 + P], ACT.Copy)
                act.activation(pT[:, 0:b + 1, :].rearrange("p j q -> p (j q)"), bank(B_T)[:, 0:(b + 1) * P], ACT.Copy)
                act.activation(pT[0:META, CH, :], bank(B_T if b < CH - 1 else B_A)[0:META, 3 * P:], ACT.Copy) \
                    .then_inc(pT_ready, 1)

            def values_out(h, b, v, done, step, ready):
                act.wait_ge(done, step)
                act.activation(v[:, 0:CH, :].rearrange("p c d -> p (c d)"), bank(b), ACT.Copy).then_inc(ready, 1)

            def split_hi(h, branch):
                act.wait_ge(og_ready, 2 * h + 3 + branch)
                act.activation((oa_hi, ob_hi)[branch][:, bass.ds(h, 1), :].rearrange("p a t -> p (a t)"),
                               og[:, :], ACT.Copy).then_inc(oghi_ready, 1)

            def head(h, last):
                def period(p):
                    if p == 0:
                        take(h, 3)
                    elif p <= SECTIONS - AHEAD:
                        take(h, p + 3)
                    elif not last:
                        take(h + 1, p - 5)
                    else:
                        gate_out(p - 5)
                    u = SECTIONS * h + 7 + p
                    convert_hi(act, u, (7 + p) % SLOTS, 2 * h + (7 + p) // SLOTS + 1)

                period(0)
                period(1)
                period(2)
                exps(h, 0)
                period(3)
                act.wait_ge(hg_done, hg(h, "keys"))
                act.activation(k_tok[:, 0:CH - 1, :].rearrange("p c d -> p (c d)"), bank(B_HG)[:, 0:(CH - 1) * P],
                               ACT.Copy)
                act.activation(k_tok[0:META, CH - 1, :], bank(B_HG)[0:META, (CH - 1) * P:], ACT.Copy) \
                    .then_inc(ktok_ready, 1)
                exps(h, 1)
                values_out(h, B_T, v_b, at_done, atn(h, "values"), vb_ready)
                values_out(h, B_HG, v_a, hg_done, hg(h, "values"), va_ready)
                probs_out(h, 0)
                period(4)
                exps(h, 2)
                square(h, 0, B_HG, hg_done, hg(h, "out"))
                probs_out(h, 1)
                period(5)
                probs_out(h, 2)
                split_hi(h, 0)
                exps(h, 3)
                period(6)
                probs_out(h, 3)
                square(h, 1, B_A, at_done, atn(h, "a3"))
                period(7)
                split_hi(h, 1)

            def gate_out(i):
                act.wait_ge(w_used, T0 + i + 1)
                if i == 0:
                    act.wait_ge(on_ready, 2 * HEADS - 1)
                act.activation(tg[:, i, :], bank(0 if i % 2 == 0 else 2), ACT.Tanh, scale=0.5) \
                    .then_inc(sec_taken, 1)

            with act.Fori(0, HEADS - 1) as h:
                head(h, False)
            head(HEADS - 1, True)
            gate_out(3)

            def merge_hi(d):
                act.wait_ge(m_sum, d + 1)
                act.activation(m_hi[:, bass.ds(d, 1), :].rearrange("p a t -> p (a t)"), t_m[:, 0, :], ACT.Copy,
                               scale=0.5).then_inc(mhi_ready, 1)

            def ahead(u, at_u, loads):
                convert_hi(act, u, at_u % SLOTS, loads)

            for u in range(T0 + 7, T0 + 9):
                ahead(u, u, u // SLOTS + 1)
            merge_hi(0)
            for u in range(T0 + 9, T0 + 11):
                ahead(u, u, u // SLOTS + 1)
            merge_hi(1)
            with act.Fori(0, KT // 2 - 1) as i:
                for dd in range(2):
                    for j in range(4):
                        at_u = T0 + 11 + 4 * dd + j
                        ahead(8 * i + at_u, at_u, 2 * i + at_u // SLOTS + 1)
                        if j in (1, 2):
                            g = j - 1
                            act.wait_ge(w_used, T0 + 8 * i + 8 + 4 * dd + g + 1)
                            act.wait_ge(y_taken, 4 * i + 2 * dd + 2 + g + 1)
                            act.activation(t_gate[:, g, :], bank(4 * dd + g), ACT.Tanh, scale=0.5) \
                                .then_inc(gate_taken, 1)
                    merge_hi(2 * i + 2 + dd)
            for u in range(O0 + 3, ALL_UNITS):
                ahead(u, u, u // SLOTS + 1)
            for j in range(2):
                for t in range(CH):
                    act.wait_ge(o_taken, CH * j + t + 1)
                    if j + t > 0:
                        act.wait_ge(o_sq, CH * j + t)
                    act.activation(y_sq[:, :], y_out[:, t, 512 * j:512 * (j + 1)], ACT.Square,
                                   accum_out=(ss, ss2)[j][:, t:t + 1]).then_inc(o_sq, 1)

        @block.vector
        def _(dve):
            own = [0]

            def pre(ins):
                own[0] += 1
                ins.then_inc(v_pre, 1)
                return own[0]

            def norm_x(n):
                i = X_ORDER[n]
                m = P if i < CH else META
                dve.wait_ge(x_rstd, n + 1)
                if n == 0:
                    dve.wait_ge(norm_in, 16)
                dve.scalar_tensor_tensor(x_in[0:m, i, :], x_in[0:m, i, :], rstd[0:m, i:i + 1], g_in[0:m, :],
                                         ALU.mult, ALU.mult).then_inc(x_normed, 1)

            def mean_x(n):
                i = X_ORDER[n]
                m = P if i < CH else META
                dve.wait_ge(x_squared, n + 1)
                dve.tensor_scalar(ms[0:m, i:i + 1], ss[0:m, i:i + 1], 1.0 / D, EPS, ALU.mult, ALU.add) \
                    .then_inc(x_ms, 1)

            def turned_x(n):
                i = X_ORDER[n]
                dve.wait_ge(u_ready_hi, n + 1)
                if i == CH:
                    dve.tensor_tensor(uT_lo[:, :, 0:META], bank(3)[:, 0:KT * META].rearrange("p (k t) -> p k t", k=KT),
                                      uT_hi[:, :, 0:META].bitcast(F32), ALU.subtract).then_inc(u_ready_lo, 1)
                    return
                for g in range(2):
                    lo, hi = (a[:, 4 * g:4 * g + 4, META + i * P:META + (i + 1) * P] for a in (uT_lo, uT_hi))
                    ins = dve.tensor_tensor(lo, bank(4 + 2 * (i % 2) + g).rearrange("p (k t) -> p k t", k=4),
                                            hi.bitcast(F32), ALU.subtract)
                ins.then_inc(u_ready_lo, 1)

            mean_x(0)
            norm_x(0)
            mean_x(1)
            norm_x(1)
            mean_x(2)
            turned_x(0)
            norm_x(2)
            mean_x(3)
            dve.wait_ge(pe_pre, 1)
            pre(dve.tensor_copy(lbt, bank(3)[:, 256:256 + 2 * HEADS + 2]))
            turned_x(1)
            norm_x(3)
            mean_x(4)
            convert_lo(dve, 0, 0)
            turned_x(2)
            norm_x(4)
            turned_x(3)
            convert_lo(dve, 1, 1)
            turned_x(4)
            convert_lo(dve, 2, 2)
            dve.wait_ge(tables_in, 64)
            pre(dve.tensor_copy(bias_bf[:, :], bias_in[:, :]))
            pre(dve.tensor_tensor(lam_pr[:, :, :], lam_in[:, 0:4:2, :], lam_in[:, 1:4:2, :], ALU.mult))
            dve.wait_ge(v_pre, 3)
            pre(dve.tensor_reduce(lam2, lam_pr[:, :, :], AX.X, ALU.add))
            pre(dve.tensor_tensor(e_m, lbt[:, 0:HEADS], lbt[:, HEADS:2 * HEADS], ALU.max))
            dve.wait_ge(v_pre, 5)
            pre(dve.tensor_tensor(e_0, lbt[:, 0:HEADS], e_m, ALU.subtract))
            pre(dve.tensor_tensor(e_1, lbt[:, HEADS:2 * HEADS], e_m, ALU.subtract))
            pre(dve.tensor_copy(ident_bf[:, :], ident[:, :]))
            pre(dve.tensor_scalar(gain_a, lbt[:, 16:17], 0.5, None, ALU.mult))
            pre(dve.tensor_scalar(gain_b, lbt[:, 17:18], 0.5 * (1.0 - LAM_INIT), None, ALU.mult))
            dve.wait_ge(a_pre, 1)
            n = pre(dve.tensor_tensor(neg_lam, lam2[:, 1:2], lam2[:, 0:1], ALU.subtract))
            dve.wait_ge(v_pre, n)
            pre(dve.tensor_scalar(neg_lam, neg_lam, LAM_INIT, None, ALU.subtract))
            dve.wait_ge(a_pre, 3)
            n = pre(dve.tensor_tensor(e_1, e_0, e_1, ALU.add))
            dve.wait_ge(v_pre, n)
            n = pre(dve.reciprocal(e_m, e_1))
            dve.wait_ge(v_pre, n)
            n = pre(dve.tensor_tensor(e_1, e_0, e_m, ALU.mult))
            dve.wait_ge(v_pre, n)
            pre(dve.tensor_scalar(f_mul, e_1, -0.5, 0.5, ALU.mult, ALU.add))
            n = pre(dve.tensor_scalar(f_neg, e_1, 0.5, -0.5, ALU.mult, ALU.add))
            dve.wait_ge(v_pre, n)
            n = pre(dve.tensor_tensor(f_add, e_1, f_mul, ALU.add))
            dve.wait_ge(v_pre, n)
            for n in range(AHEAD):
                convert_lo(dve, n + 3, (n + 3) % SLOTS)

            t_of, at_ = {1: f[:, :]}, 0
            for m in (2, 4, 8, 16, 32, 64, 128):
                n = TOK // m if m <= META else SEQ // m
                t_of[m] = tt[:, at_:at_ + n]
                at_ += n
            OWN = 48

            def head(h):
                count = [0]

                def chained():
                    dve.wait_ge(dve_own, OWN * h + count[0])

                def mark(ins):
                    count[0] += 1
                    ins.then_inc(dve_own, 1)

                def chain(ins):
                    mark(ins)
                    chained()

                def conv(p):
                    convert_lo(dve, SECTIONS * h + 7 + p, (7 + p) % SLOTS)

                def gate(branch):
                    dve.wait_ge(sec_taken, SECTIONS * h + 6 + 2 * branch)
                    dve.scalar_tensor_tensor((gate_a, gate_b)[branch][:, :], th_z[:, :], 1.0, z_g[:, :], ALU.add,
                                             ALU.mult).then_inc(gate_ready, 1)

                def next_level(m):
                    e = LEVELS.index(m) + 1
                    if m > 1:
                        chained()
                    dve.wait_ge(lvl_taken, 8 * h + e)
                    dve.wait_ge(hg_done, hg(h, f"l{m}"))
                    if m < META:
                        kv = kk[:, :].rearrange("p (b two m) -> p b two m", two=2, m=m)
                        tk = t_of[m].rearrange("p (b two) -> p b two", two=2)
                        tq = tk[:, META // (2 * m):, :]
                    else:
                        kv = kk[:, META:].rearrange("p (b two m) -> p b two m", two=2, m=m)
                        t = t_of[m][:, 1:] if m == META else t_of[m]
                        tk = tq = t.rearrange("p (b two) -> p b two", two=2)
                    qv = qq[:, :].rearrange("p (b two m) -> p b two m", two=2, m=m)
                    nk, nq = kv.shape[1], qv.shape[1]
                    dve.tensor_tensor(kv[:, :, 0, :], kv[:, :, 0, :],
                                      tk[:, :, 1:2].to_broadcast([P, nk, m]), ALU.mult)
                    dve.tensor_tensor(qv[:, :, 1, :], qv[:, :, 1, :],
                                      tq[:, :, 0:1].to_broadcast([P, nq, m]), ALU.mult).then_inc(lvl_ready, 1)
                    mark(dve.tensor_tensor(t_of[2 * m], tk[:, :, 0], tk[:, :, 1], ALU.mult))

                def take_level(e):
                    src = bank(B_HG)
                    if e == 0:
                        dve.wait_ge(hg_done, hg(h, "diag"))
                        dve.tensor_tensor(aa[:, :, :], src.rearrange("p (c t) -> p c t", c=CH),
                                          ident[:, :].rearrange("p (a t) -> p a t", a=1).to_broadcast([P, CH, P]),
                                          ALU.mult).then_inc(lvl_taken, 1)
                    elif e <= MASKED:
                        m = LEVELS[e - 1]
                        for c in range(CH):
                            dst = aa[:, c, :].rearrange("p (b two m) -> p b two m", two=2, m=m)[:, :, 1, :]
                            ins = dve.copy_predicated(
                                dst, masks[:, e - 1, :].rearrange("p (b m) -> p b m", m=m),
                                src[:, c * 64:(c + 1) * 64].rearrange("p (b m) -> p b m", m=m))
                        ins.then_inc(lvl_taken, 1)
                    else:
                        dve.tensor_copy(v_a[0:META, CH, :], src[0:META, 256:256 + P])
                        dve.tensor_copy(aa[0:64, :, 64:128],
                                        src[0:64, 0:CH * 64].rearrange("p (c t) -> p c t", c=CH)) \
                            .then_inc(lvl_taken, 1)

                def step_level(e):
                    next_level(LEVELS[e - 1])
                    take_level(e)

                def norm(branch, b):
                    dve.wait_ge(o_squared, 2 * h + branch + 1)
                    chain(dve.tensor_reduce(ss[:, 0:CH], sq[:, :, :], AX.X, ALU.add))
                    dve.tensor_scalar(ms[:, 0:CH], ss[:, 0:CH], 1.0 / P, EPS, ALU.mult, ALU.add) \
                        .then_inc(ms_ready, 1)
                    dve.wait_ge(rstd_ready, 2 * h + branch + 1)
                    r = rstd[:, 0:CH].rearrange("p (c a) -> p c a", a=1).to_broadcast([P, CH, P])
                    dve.tensor_tensor(on[:, :, :], bank(b).rearrange("p (c d) -> p c d", c=CH), r,
                                      ALU.mult).then_inc(on_ready, 1)

                def gated(branch):
                    dve.wait_ge(*((hg_done, hg(h, "turn")) if branch == 0 else (at_done, atn(h, "turn"))))
                    dve.wait_ge(oghi_ready, 2 * h + branch + 2)
                    dve.tensor_tensor(og[:, :], bank((B_HG, B_T)[branch]), (gate_a, gate_b)[branch][:, :], ALU.mult) \
                        .then_inc(og_ready, 1)

                def split_lo(branch):
                    hi, lo = ((oa_hi, oa_lo), (ob_hi, ob_lo))[branch]
                    dve.wait_ge(oghi_ready, 2 * h + branch + 3)
                    at_h = bass.ds(h, 1)
                    dve.tensor_tensor(lo[:, at_h, :].rearrange("p a t -> p (a t)"), og[:, :],
                                      hi[:, at_h, :].rearrange("p a t -> p (a t)").bitcast(F32), ALU.subtract) \
                        .then_inc(oglo_ready, 1)

                def swap_pairs(t):
                    swap = [i + 8 if i < 8 else i - 8 if i < 16 else i for i in range(32)]
                    mark(dve.stream_shuffle(shuf[:, 0:t.shape[1]], t, swap))

                def turn_pairs(t, lo):
                    n = t.shape[1]
                    chained()
                    dve.tensor_tensor(t, t, rope[:, 0, lo:lo + n], ALU.mult)
                    mark(dve.tensor_tensor(shuf[:, 0:n], shuf[:, 0:n], rope[:, 1, lo:lo + n], ALU.mult))

                def add_pairs(t):
                    chained()
                    return dve.tensor_tensor(t, t, shuf[:, 0:t.shape[1]], ALU.add)

                def row_max(b):
                    n = min(n_keys(b), 512)
                    dve.wait_ge(at_done, atn(h, f"s{b}"))
                    if b == CH - 1:
                        dve.tensor_reduce(mx2, bank(B_T)[:, 0:2 * META].rearrange("p (c n) -> p c n", c=2), AX.X,
                                          ALU.max)
                    chain(dve.tensor_reduce(mx, ps[:, B_S:B_S + 2, 0:n], AX.X, ALU.max))
                    if b == CH - 1:
                        chain(dve.tensor_tensor(mx, mx, mx2, ALU.max))
                    dve.tensor_scalar(nb, mx, -SCALE, None, ALU.mult).then_inc(nb_ready, 1)

                def probs(b):
                    n = n_keys(b)
                    a1, a2 = e1[:, b % 2, 0:n], e2[:, b % 2, 0:n]
                    dve.wait_ge(exp_done, 8 * h + 2 * b + 2)
                    if b == CH - 1:
                        chain(dve.tensor_tensor(lsum, lsum, lsum2, ALU.add))
                    chain(dve.reciprocal(rl, lsum))
                    dve.tensor_tensor(rl[:, 1:2], rl[:, 1:2], neg_lam, ALU.mult)
                    chain(dve.tensor_scalar(a1, a1, rl[:, 0:1], None, ALU.mult))
                    dve.scalar_tensor_tensor(a1, a2, rl[:, 1:2], a1, ALU.mult, ALU.add).then_inc(p_ready, 1)

                hcol = bass.ds(h, 1)
                dve.wait_ge(sec_taken, SECTIONS * h + 2)
                dve.wait_ge(hg_done, hg(h - 1, "out"))
                dve.tensor_scalar(f[:, :], kk[:, :], f_mul[:, hcol], f_add[:, hcol], ALU.mult, ALU.add)
                chain(dve.tensor_scalar(kk[:, :], kk[:, :], f_neg[:, hcol], f_mul[:, hcol], ALU.mult, ALU.add))
                dve.tensor_tensor(qq[:, :], q_raw[:, :], f[:, META:], ALU.mult).then_inc(k_ready, 1)
                dve.wait_ge(sec_taken, SECTIONS * h + 3)
                conv(0)
                swap_pairs(kT[:, :])
                take_level(0)
                turn_pairs(kT[:, :], 0)
                dve.wait_ge(sec_taken, SECTIONS * h + 4)
                step_level(1)
                mark(add_pairs(kT[:, :]))
                step_level(2)
                swap_pairs(qT[:, :])
                step_level(3)
                turn_pairs(qT[:, :], META)
                step_level(4)
                add_pairs(qT[:, :]).then_inc(rope_ready, 1)
                step_level(5)
                conv(1)
                step_level(6)
                row_max(0)
                probs(0)
                step_level(7)
                row_max(1)
                conv(2)
                probs(1)
                gate(0)
                dve.wait_ge(hg_done, hg(h, "sums"))
                chain(dve.tensor_copy(st[:, 0, :], bank(B_HG)[:, 0:P]))
                for c in range(CH - 1):
                    ins = dve.scalar_tensor_tensor(st[:, c + 1, :], st[:, c, :], t_of[128][:, c:c + 1],
                                                   bank(B_HG)[:, (c + 1) * P:(c + 2) * P], ALU.mult, ALU.add)
                    if c < CH - 2:
                        chain(ins)
                    else:
                        ins.then_inc(st_ready, 1)
                row_max(2)
                norm(0, B_HG)
                probs(2)
                conv(3)
                conv(4)
                gated(0)
                gate(1)
                row_max(3)
                split_lo(0)
                conv(5)
                probs(3)
                conv(6)
                norm(1, B_A)
                conv(7)
                gated(1)
                split_lo(1)
                assert count[0] <= OWN, count
                if count[0] < OWN:
                    dve.sem_inc(dve_own, OWN - count[0])

            with dve.Fori(0, HEADS - 1) as h:
                head(h)
            head(HEADS - 1)

            def merge(d, last_u, gates, banks):
                dve.wait_ge(mlo_ready, d) if not isinstance(d, int) or d > 0 else None
                for b in range(2):
                    dve.wait_ge(w_used, last_u + b)
                    dve.scalar_tensor_tensor(t_m[:, b, :], gates[:, b, :], 1.0, bank(banks + b),
                                             ALU.add, ALU.mult).then_inc(y_taken, 1)
                dve.wait_ge(y_taken, 2 * d + 2)
                dve.tensor_tensor(t_m[:, 0, :], t_m[:, 0, :], t_m[:, 1, :], ALU.add).then_inc(m_sum, 1)

            def merge_lo(d):
                dve.wait_ge(mhi_ready, d + 1)
                at_d = bass.ds(d, 1)
                dve.scalar_tensor_tensor(m_lo[:, at_d, :].rearrange("p a t -> p (a t)"), t_m[:, 0, :], 0.5,
                                         m_hi[:, at_d, :].rearrange("p a t -> p (a t)").bitcast(F32),
                                         ALU.mult, ALU.subtract).then_inc(mlo_ready, 1)

            convert_lo(dve, T0 + 7, (T0 + 7) % SLOTS)
            convert_lo(dve, T0 + 8, (T0 + 8) % SLOTS)
            merge(0, T0 + 5, tg[:, 0:2, :], 2)
            convert_lo(dve, T0 + 9, (T0 + 9) % SLOTS)
            merge_lo(0)
            convert_lo(dve, T0 + 10, (T0 + 10) % SLOTS)
            merge(1, T0 + 7, tg[:, 2:4, :], 6)
            merge_lo(1)
            with dve.Fori(0, KT // 2 - 1) as i:
                for dd in range(2):
                    for j in range(4):
                        at_u = T0 + 11 + 4 * dd + j
                        convert_lo(dve, 8 * i + at_u, at_u % SLOTS)
                    dve.wait_ge(gate_taken, 4 * i + 2 * dd + 6)
                    merge(2 * i + 2 + dd, T0 + 8 * i + 8 + 4 * dd + 3, t_gate, 4 * dd + 2)
                    merge_lo(2 * i + 2 + dd)
            for u in range(O0 + 3, ALL_UNITS):
                convert_lo(dve, u, u % SLOTS)
            dve.wait_ge(xres_loaded, 16 * (CH + 1))
            def add_x(j, t):
                if t < CH - 1:
                    dve.wait_ge(o_done, (CH - 1) * j + t + 1)
                else:
                    dve.wait_ge(w_used, O0 + 4 * j + 4)
                dve.tensor_tensor(y_out[:, t, 512 * j:512 * (j + 1)], bank(4 * j + t),
                                  x_res[:, t, 512 * j:512 * (j + 1)], ALU.add).then_inc(o_taken, 1)
            def mean(t):
                dve.wait_ge(o_sq, CH + t + 1)
                dve.tensor_tensor(ss[:, t:t + 1], ss[:, t:t + 1], ss2[:, t:t + 1], ALU.add).then_inc(o_own, 1)
                dve.wait_ge(o_own, t + 1)
                dve.tensor_scalar(ms[:, t:t + 1], ss[:, t:t + 1], 1.0 / D, EPS, ALU.mult, ALU.add).then_inc(o_ms, 1)
            def finish(t):
                dve.wait_ge(o_rstd, t + 1)
                dve.scalar_tensor_tensor(y_out[:, t, :], y_out[:, t, :], rstd[:, t:t + 1], g_fin[:, :], ALU.mult,
                                         ALU.mult).then_inc(y_ready, 1)
            for t in range(CH):
                add_x(0, t)
            for t in range(CH):
                add_x(1, t)
                if t > 0:
                    mean(t - 1)
                if t > 1:
                    finish(t - 2)
            mean(CH - 1)
            finish(CH - 2)
            finish(CH - 1)


_INS = ["x", "meta_tokens", "norm_g", "w_in", "hg_lb_logits", "hg_norm_g", "da_lambda", "da_norm_g",
        "w_branch_a", "w_branch_b", "w_out", "final_g"]


def kernel(**inputs):
    import concourse.bacc as bacc
    from concourse.bass_utils import run_bass_kernel_spmd as run

    nc = bacc.Bacc("TRN2", target_bir_lowering=False, num_devices=1)
    arrays, args = {}, []
    laid = {n: np.ascontiguousarray(inputs[n]) for n in _INS}
    laid.update(constants())
    for name, a in laid.items():
        arrays[f"in_{name}"] = a
        args.append(nc.dram_tensor(f"in_{name}", a.shape, mybir.dt.from_np(a.dtype), kind="ExternalInput").ap())
    args.append(nc.dram_tensor("out_0", (1, SEQ, D), F32, kind="ExternalOutput").ap())
    build(nc, *args)
    r = run(nc, [arrays], core_ids=[0])
    return r.results[0]["out_0"]
```

```python
import numpy as np
import concourse.bass as bass
from concourse import mybir

F32 = mybir.dt.float32
F32R = mybir.dt.float32r
BF16 = mybir.dt.bfloat16
U32 = mybir.dt.uint32
ALU = mybir.AluOpType
ACT = mybir.ActivationFunctionType
AX = mybir.AxisListType

P = 128
D = 1024
SEQ = 512
META = 16
TOK = META + SEQ
KT = D // P
HEADS = D // P
CH = SEQ // P
NT = CH + 1
EPS = 1e-6
LAM_INIT = 0.2
DA_D = 64
SCALE = DA_D ** -0.5
ROPE_DIM = DA_D // 4
ROPE_THETA = 500000.0
NEG = -1e30
LEVELS = [1 << i for i in range(7)]
MASKED = 5
X_ORDER = (0, 1, CH, 2, 3)
HQ, HF, HI, HZ, AQ, AK, AV, AZ, GA, GB = (i * D for i in range(10))

UNIT = 1024
SLOTS = 4
RAW = 2
SECTIONS = 8
COLS = (HF, HQ, AK, AQ, HI, HZ, AV, AZ)
AHEAD = 4
T0 = SECTIONS * HEADS
T_UNITS = 4 * KT
O0 = T0 + T_UNITS
ALL_UNITS = O0 + 8

HG_STEPS = ["l1", "l2", "l4", "l8", "l16", "l32", "l64", "keys", "values", "sums", "out", "turn"]
AT_STEPS = ["s0", "s1", "values", "t0", "s2", "a0", "t1", "a1", "t2", "s3", "a2", "t3", "a3", "turn"]
HG, AT = len(HG_STEPS), len(AT_STEPS)
HG_AT = dict(zip(HG_STEPS, (3, 8, 11, 14, 17, 20, 23, 26, 29, 32, 35, 40)))
AT_AT = dict(zip(AT_STEPS, (22, 26, 29, 31, 32, 34, 37, 39, 42, 44, 46, 52, 54, 60)))


def constants():
    ident = np.eye(P, dtype=np.float32)
    q, k = np.arange(P)[:, None], np.arange(P)[None, :]
    bias = np.where(k <= q, np.float32(0), np.float32(NEG)).astype(np.float32)
    masks = np.zeros((P, MASKED, P // 2), np.uint32)
    s = np.arange(P)[:, None]
    j = np.arange(P // 2)[None, :]
    for i, m in enumerate(LEVELS[:MASKED]):
        t = (j // m) * 2 * m + m + j % m
        masks[:, i, :] = (s // (2 * m) == t // (2 * m)) & (s % (2 * m) < m)
    half = ROPE_DIM // 2
    inv = np.float32(ROPE_THETA) ** (-np.arange(half, dtype=np.float32) * np.float32(2.0) / np.float32(ROPE_DIM))
    ang = np.arange(TOK, dtype=np.float32)[None, :] * inv.astype(np.float32)[:, None]
    cos, sin = np.cos(ang), np.sin(ang)
    rope = np.zeros((P, 2, TOK), np.float32)
    rope[:, 0, :] = 1.0
    for c in (0, DA_D):
        rope[c:c + half, 0], rope[c + half:c + ROPE_DIM, 0] = cos, cos
        rope[c:c + half, 1], rope[c + half:c + ROPE_DIM, 1] = -sin, sin
    return {"c_ident": ident, "c_bias": bias, "c_masks": masks, "c_rope": rope}


def build(nc, x, meta_tokens, norm_g, w_in, lb_logits, hg_norm_g, da_lambda, da_norm_g,
          w_branch_a, w_branch_b, w_out, final_g, c_ident, c_bias, c_masks, c_rope, out):
    x = x.rearrange("b s d -> (b s) d")
    out = out.rearrange("b s d -> (b s) d")
    w_in = w_in.rearrange("l (k p) n -> p (l k) n", p=P)
    w_branch_a = w_branch_a.rearrange("l (k p) n -> p (l k) n", p=P)
    w_branch_b = w_branch_b.rearrange("l (k p) n -> p (l k) n", p=P)
    w_out = w_out.rearrange("l (k p) n -> p (l k) n", p=P)

    def at(name, shape, dt, offset):
        size = int(np.prod(shape[1:])) * (2 if dt == BF16 else 4)
        return nc.alloc_sbuf_tensor_at(name, shape, dt, offset=offset), offset + (size + 31) // 32 * 32

    base = 16512
    uT_hi, o = at("uT_hi", [P, KT, TOK], F32R, base)
    uT_lo, o = at("uT_lo", [P, KT, TOK], F32R, o)
    w_raw, o = at("w_raw", [P, RAW, UNIT], F32, o)
    w_hi, o = at("w_hi", [P, SLOTS, UNIT], F32R, o)
    w_lo, o = at("w_lo", [P, SLOTS, UNIT], F32R, o)
    region_o = o
    x_in, o2 = at("x_in", [P, NT, D], F32, region_o)
    g_in, o2 = at("g_in", [P, D], F32, o2)
    x_sq, o2 = at("x_sq", [P, D], F32, o2)
    oa_hi, o = at("oa_hi", [P, KT, SEQ], F32R, region_o)
    oa_lo, o = at("oa_lo", [P, KT, SEQ], F32R, o)
    ob_hi, o = at("ob_hi", [P, KT, SEQ], F32R, o)
    ob_lo, o = at("ob_lo", [P, KT, SEQ], F32R, o)
    y_out, o3 = at("y_out", [P, CH, D], F32, region_o)
    y_sq, o3 = at("y_sq", [P, SEQ], F32, o3)
    ident, o = at("ident", [P, P], F32, o)
    ident_bf, o = at("ident_bf", [P, P], BF16, o)
    bias_bf, o = at("bias_bf", [P, P], BF16, o)
    masks, o = at("masks", [P, MASKED, P // 2], U32, o)
    rope, o = at("rope", [P, 2, TOK], F32, o)
    small, o = at("small", [P, 128], F32, o)
    region_w = o
    f, o = at("f", [P, TOK], F32, o)
    tt, o = at("tt", [P, TOK], F32, o)
    q_1, o = at("q_1", [P, CH, P + P // 2], F32, o)
    aa, o = at("aa", [P, CH, P], F32, o)
    tg, _ = at("tg", [P, 4, SEQ], F32, region_w)
    region_m = o
    kk, o = at("kk", [P, TOK], F32, o)
    qq, o = at("qq", [P, SEQ], F32, o)
    k_tok, o = at("k_tok", [P, CH, P], F32, o)
    st, o = at("st", [P, CH, P], F32, o)
    sq, o = at("sq", [P, CH, P], F32, o)
    k_first = sq[:, 0:2, :].rearrange("p c t -> p (c t)")
    on, o = at("on", [P, CH, P], F32, o)
    og, o = at("og", [P, SEQ], F32, o)
    th_z, o = at("th_z", [P, SEQ], F32, o)
    z_g, o = at("z_g", [P, SEQ], F32, o)
    gate_a, o = at("gate_a", [P, SEQ], F32, o)
    gate_b, o = at("gate_b", [P, SEQ], F32, o)
    kT, o = at("kT", [P, TOK], F32, o)
    qT, o = at("qT", [P, SEQ], F32, o)
    pT, o = at("pT", [P, NT, P], F32, o)
    v_b, o = at("v_b", [P, NT, P], F32, o)
    kT_hi, o = at("kT_hi", [P, TOK], F32R, o)
    kT_lo, o = at("kT_lo", [P, TOK], F32R, o)
    qT_hi, o = at("qT_hi", [P, SEQ], F32R, o)
    qT_lo, o = at("qT_lo", [P, SEQ], F32R, o)
    e1, o = at("e1", [P, 2, TOK], F32, o)
    e2, o = at("e2", [P, 2, TOK], F32, o)
    shuf = e2[:, 1, :]
    vT_a, o = at("vT_a", [P, TOK], F32, o)
    vT_b, o = at("vT_b", [P, TOK], F32, o)
    v_a, o = at("v_a", [P, NT, P], F32, o)
    assert o <= 229344
    lam_in, _ = at("lam_in", [P, 4, DA_D], F32, region_w)
    rows_in, _ = at("rows_in", [2 * HEADS + 2, P], F32, region_w + 4096)
    bias_in, _ = at("bias_in", [P, P], F32, region_w + 8192)
    lam_pr, _ = at("lam_pr", [P, 2, DA_D], F32, region_w + 12288)
    m_hi, o2 = at("m_hi", [P, KT, SEQ], F32R, region_m)
    m_lo, o2 = at("m_lo", [P, KT, SEQ], F32R, o2)
    t_gate, o2 = at("t_gate", [P, 2, SEQ], F32, o2)
    t_m, o2 = at("t_m", [P, 2, SEQ], F32, o2)
    x_res, o3 = at("x_res", [P, CH, D], F32, base)
    g_fin, o3 = at("g_fin", [P, D], F32, o3)

    taken = [0]

    def cols(n):
        taken[0] += n
        return small[:, taken[0] - n:taken[0]]

    lbt = cols(2 * HEADS + 2)
    f_mul, f_neg, f_add, e_0, e_1, e_m = (cols(HEADS) for _ in range(6))
    gain_a, gain_b, neg_lam, lam2, warm = cols(1), cols(1), cols(1), cols(2), cols(NT)
    ss, ms, rstd, half_neg, ss2 = (cols(NT) for _ in range(5))
    mx, nb, lsum, rl, mx2, lsum2 = (cols(2) for _ in range(6))

    ps = nc.alloc_psum_tensor("ps", [P, 8, 512], F32)

    def bank(i):
        return ps[:, i, :]

    B_HG, B_S, B_T, B_A = 3, 4, 6, 7
    PAIR = ps[:, 0:2, 0:TOK // 2]

    def level_bank(e):
        return B_S + 1 if e in (2, 4) else B_HG

    sem = nc.alloc_semaphore
    ident_in, norm_in, meta_in, rows_ready, tables_in = (sem(n) for n in (
        "ident_in", "norm_in", "meta_in", "rows_ready", "tables_in"))
    x_loaded = [sem(f"x_loaded{i}") for i in range(CH)]
    xres_loaded, stored = sem("xres_loaded"), sem("stored")
    w_loaded = [sem(f"w_loaded{i}") for i in range(RAW)]
    slot_free = sem("slot_free")
    hi_ready, lo_ready, w_used = sem("hi_ready"), sem("lo_ready"), sem("w_used")
    v_pre, a_pre, g_pre, pe_pre = sem("v_pre"), sem("a_pre"), sem("g_pre"), sem("pe_pre")
    u_ready_hi, u_ready_lo = sem("u_ready_hi"), sem("u_ready_lo")
    x_squared, x_ms, x_rstd, x_normed, x_turned = (sem(n) for n in (
        "x_squared", "x_ms", "x_rstd", "x_normed", "x_turned"))
    sec_taken = sem("sec_taken")
    dve_own = sem("dve_own")
    k_ready, lvl_ready, lvl_taken = sem("k_ready"), sem("lvl_ready"), sem("lvl_taken")
    hg_done, at_done = sem("hg_done"), sem("at_done")
    ktok_ready, va_ready, st_ready = sem("ktok_ready"), sem("va_ready"), sem("st_ready")
    vb_ready = sem("vb_ready")
    rotated, rothi_ready = sem("rotated"), sem("rothi_ready")
    o_squared, ms_ready, rstd_ready, on_ready, og_ready, oghi_ready, oglo_ready = (sem(n) for n in (
        "o_squared", "ms_ready", "rstd_ready", "on_ready", "og_ready", "oghi_ready", "oglo_ready"))
    rope_ready, gate_ready = sem("rope_ready"), sem("gate_ready")
    meta_scored = sem("meta_scored")
    nb_ready, exp_done, p_ready, pT_ready = sem("nb_ready"), sem("exp_done"), sem("p_ready"), sem("pT_ready")
    gate_taken, y_taken, m_sum, mhi_ready, mlo_ready = (sem(n) for n in (
        "gate_taken", "y_taken", "m_sum", "mhi_ready", "mlo_ready"))
    o_done, o_taken, o_sq, o_half, o_gained, o_ms, o_rstd, y_left, y_right = (sem(n) for n in (
        "o_done", "o_taken", "o_sq", "o_half", "o_gained", "o_ms", "o_rstd", "y_left", "y_right"))

    def convert_hi(act, u, slot, loads):
        act.wait_ge(w_loaded[slot % RAW], 16 * loads)
        if not isinstance(u, int) or u >= SLOTS:
            act.wait_ge(w_used, u - SLOTS + 1)
        act.activation(w_hi[:, slot, :], w_raw[:, slot % RAW, :], ACT.Copy).then_inc(hi_ready, 1)

    def convert_lo(eng, u, slot):
        eng.wait_ge(hi_ready, u + 1)
        eng.tensor_tensor(w_lo[:, slot, :], w_raw[:, slot % RAW, :], w_hi[:, slot, :].bitcast(F32),
                          ALU.subtract).then_inc(lo_ready, 1)

    def hg(h, step):
        return HG * (h + 1) + HG_STEPS.index(step) + 1

    def atn(h, step):
        return AT * (h + 1) + AT_STEPS.index(step) + 1

    def n_keys(b):
        return META + (b + 1) * P

    block = nc.Block()
    with block:
        @block.sync
        def _(sp):
            def load(u, slot, src):
                if not isinstance(u, int):
                    sp.wait_ge(lo_ready, u - RAW + 1)
                    sp.sem_inc(slot_free, 1)
                elif u >= RAW:
                    sp.wait_ge(lo_ready, u - RAW + 1)
                slot = slot % RAW
                sp.dma_start(w_raw[:, slot, :].rearrange("p (k n) -> p k n", k=src.shape[1]), src) \
                    .then_inc(w_loaded[slot], 16)

            def section(h, s, u, slot):
                load(u, slot, w_in[:, :, bass.ds(h * P + COLS[s], P)])

            for i in range(CH):
                sp.dma_start(x_in[:, i, :], x[i * P:(i + 1) * P, :]).then_inc(x_loaded[i], 16)
                if i == 1:
                    section(0, 0, 0, 0)
            section(0, 1, 1, 1)
            sp.dma_start(rows_in[0:2 * HEADS, :], lb_logits.rearrange("r (h p) -> (r h) p", p=P)) \
                .then_inc(rows_ready, 16)
            sp.dma_start(rows_in[2 * HEADS:2 * HEADS + 1, :], hg_norm_g).then_inc(rows_ready, 16)
            sp.dma_start(rows_in[2 * HEADS + 1:2 * HEADS + 2, :], da_norm_g).then_inc(rows_ready, 16)
            sp.dma_start(lam_in[:, :, :].rearrange("p r d -> p (r d)"),
                         da_lambda.rearrange("l r d -> l (r d)").to_broadcast([P, 4 * DA_D])) \
                .then_inc(tables_in, 16)
            sp.dma_start(bias_in[:, :], c_bias).then_inc(tables_in, 16)
            sp.dma_start(masks[:, :, :], c_masks).then_inc(tables_in, 16)
            sp.dma_start(rope[:, :, :], c_rope).then_inc(tables_in, 16)
            section(0, 2, 2, 2)
            section(0, 3, 3, 3)
            with sp.Fori(0, HEADS - 1) as h:
                for p in range(SECTIONS):
                    section(h if p < 4 else h + 1, (p + 4) % 8, SECTIONS * h + AHEAD + p, p % 4)
            for p in range(SECTIONS - AHEAD):
                section(HEADS - 1, AHEAD + p, T0 - 4 + p, p)
            for d in range(2):
                for j, col in enumerate((GA, GB)):
                    load(T0 + 2 * d + j, 2 * d + j, w_in[:, :, col + d * P:col + (d + 1) * P])
            for d in range(2):
                for j, w in enumerate((w_branch_a, w_branch_b)):
                    load(T0 + 4 + 2 * d + j, 2 * d + j, w[:, :, d * P:(d + 1) * P])
            with sp.Fori(0, KT // 2 - 1) as i:
                for dd in range(2):
                    u = T0 + 8 + 8 * i + 4 * dd
                    at_d = i * (2 * P) + (2 + dd) * P
                    load(u, 0, w_in[:, :, bass.ds(at_d + GA, P)])
                    load(u + 1, 1, w_in[:, :, bass.ds(at_d + GB, P)])
                    load(u + 2, 2, w_branch_a[:, :, bass.ds(at_d, P)])
                    load(u + 3, 3, w_branch_b[:, :, bass.ds(at_d, P)])
            for c in range(4):
                load(O0 + c, c, w_out[:, 2 * c:2 * c + 2, 0:512])
            sp.wait_ge(w_used, O0 - 2)
            for i in range(CH):
                sp.dma_start(x_res[:, i, :], x[i * P:(i + 1) * P, :]).then_inc(xres_loaded, 16)
            sp.dma_start(g_fin[:, :], final_g.rearrange("(a n) -> a n", a=1).to_broadcast([P, D])) \
                .then_inc(xres_loaded, 16)
            for c in range(4):
                load(O0 + 4 + c, c, w_out[:, 2 * c:2 * c + 2, 512:1024])
            for i in range(CH):
                for half, ready in enumerate((y_left, y_right)):
                    sp.wait_ge(ready, i + 1)
                    sp.dma_start(out[i * P:(i + 1) * P, 512 * half:512 * (half + 1)],
                                 y_out[:, i, 512 * half:512 * (half + 1)]).then_inc(stored, 16)
            sp.wait_ge(stored, 16 * 2 * CH)

        @block.gpsimd
        def _(pool):
            pool.memset(half_neg, -0.5).then_inc(g_pre, 1)
            pool.wait_ge(g_pre, 1)
            for n, i in enumerate(X_ORDER):
                m = P if i < CH else META
                pool.wait_ge(x_ms, n + 1)
                pool.tensor_tensor(rstd[0:m, i:i + 1], ms[0:m, i:i + 1], half_neg[0:m, 0:1], ALU.pow) \
                    .then_inc(x_rstd, 1)
            with pool.Fori(0, 2 * HEADS) as b:
                pool.wait_ge(ms_ready, b + 1)
                pool.tensor_tensor(rstd[:, 0:CH], ms[:, 0:CH], half_neg[:, 0:CH], ALU.pow).then_inc(rstd_ready, 1)
            for t in range(CH):
                pool.wait_ge(o_ms, t + 1)
                pool.tensor_tensor(rstd[:, t:t + 1], ms[:, t:t + 1], half_neg[:, 0:1], ALU.pow).then_inc(o_rstd, 1)

        @block.tensor
        def _(pe):
            def three(dst, w, rhs, start, stop):
                pe.matmul(dst, w[0], rhs[0], start=start, stop=False, skip_group_check=True)
                pe.matmul(dst, w[0], rhs[1], start=False, stop=False, skip_group_check=True)
                return pe.matmul(dst, w[1], rhs[0], start=False, stop=stop, skip_group_check=True)

            def turn_x(n):
                i = X_ORDER[n]
                pe.wait_ge(x_normed, n + 1)
                if i == CH:
                    pe.wait_ge(v_pre, 1)
                elif n > 2:
                    pe.wait_ge(u_ready_lo, n - 2)
                for k in range(KT):
                    if i == CH:
                        t = pe.transpose(bank(3)[:, k * META:(k + 1) * META], x_in[0:META, CH, k * P:(k + 1) * P],
                                         ident[0:META, 0:META])
                    else:
                        t = pe.transpose(bank(4 + 2 * (i % 2) + k // 4)[:, (k % 4) * P:(k % 4 + 1) * P],
                                         x_in[:, i, k * P:(k + 1) * P], ident[:, :])
                t.then_inc(x_turned, 1)

            def groups(n, s, slot, ks):
                if ks[0] == 0:
                    pe.wait_ge(lo_ready, n + 1)
                    if not isinstance(n, int) or n >= 2:
                        pe.wait_ge(sec_taken, n - 1)
                for k in ks:
                    w = tuple(a[:, slot, k * P:(k + 1) * P] for a in (w_hi, w_lo))
                    if s % 2 == 0:
                        for b in range(2):
                            rhs = tuple(a[:, k, b * (TOK // 2):(b + 1) * (TOK // 2)] for a in (uT_hi, uT_lo))
                            last = three(PAIR[:, b, :], w, rhs, k == 0, k == KT - 1)
                    else:
                        rhs = tuple(a[:, k, META:TOK] for a in (uT_hi, uT_lo))
                        last = three(bank(2), w, rhs, k == 0, k == KT - 1)
                    if k == KT - 1:
                        last.then_inc(w_used, 1)

            def merge_gate(i, ks):
                n = T0 + i
                if ks[0] == 0:
                    pe.wait_ge(lo_ready, n + 1)
                    pe.wait_ge(sec_taken, n - 1)
                for k in ks:
                    w = tuple(a[:, i, k * P:(k + 1) * P] for a in (w_hi, w_lo))
                    rhs = tuple(a[:, k, META:TOK] for a in (uT_hi, uT_lo))
                    last = three(bank(0 if i % 2 == 0 else 2), w, rhs, k == 0, k == KT - 1)
                if ks[-1] == KT - 1:
                    last.then_inc(w_used, 1)

            def half_section(s, half):
                n = (TOK if s == 0 else SEQ) // 2
                dst = PAIR[:, half, :] if s == 0 else bank(2)[:, half * n:(half + 1) * n]
                at_t = half * n + TOK - 2 * n
                pe.wait_ge(lo_ready, s + 1)
                pe.wait_ge(u_ready_lo, (3, NT)[half])
                for k in range(KT):
                    last = three(dst, tuple(a[:, s, k * P:(k + 1) * P] for a in (w_hi, w_lo)),
                                 tuple(a[:, k, at_t:at_t + n] for a in (uT_hi, uT_lo)), k == 0, k == KT - 1)
                if half == 1:
                    last.then_inc(w_used, 1)

            pe.wait_ge(ident_in, 16)
            turn_x(0)
            turn_x(1)
            pe.wait_ge(rows_ready, 48)
            pe.transpose(bank(3)[:, 256:256 + 2 * HEADS + 2], rows_in[:, :], ident[0:2 * HEADS + 2, 0:2 * HEADS + 2]) \
                .then_inc(pe_pre, 1)
            turn_x(2)
            turn_x(3)
            half_section(0, 0)
            turn_x(4)
            half_section(1, 0)
            half_section(0, 1)
            half_section(1, 1)
            for s in range(2, AHEAD):
                groups(s, s, s, range(KT))

            def level(h, e):
                dst = bank(level_bank(e))
                if e == 1:
                    pe.wait_ge(k_ready, h + 1)
                    for c in range(CH):
                        mm = pe.matmul(ps[:, B_HG + c // 2, (c % 2) * 192:(c % 2 + 1) * 192],
                                       kk[:, META + c * P:META + (c + 1) * P], q_1[:, c, :], start=True, stop=True)
                    mm.then_inc(hg_done, 1)
                    return
                pe.wait_ge(lvl_ready, 7 * h + e - 1)
                if e > 2:
                    last = e - 1 if level_bank(e - 1) == level_bank(e) else e - 2
                    pe.wait_ge(lvl_taken, 7 * h + last)
                if e == 7:
                    pe.wait_ge(sec_taken, SECTIONS * h + 5)
                    pe.transpose(dst[0:META, 256:256 + P], vT_a[:, 0:META], ident[:, :])
                m = LEVELS[e - 1]
                if e <= MASKED:
                    for c in range(CH):
                        second = qq[:, c * P:(c + 1) * P].rearrange("p (b two m) -> p b two m", two=2, m=m)
                        mm = pe.matmul(dst[:, c * 64:(c + 1) * 64].rearrange("p (b m) -> p b m", m=m),
                                       kk[:, META + c * P:META + (c + 1) * P], second[:, :, 1, :],
                                       start=True, stop=True)
                else:
                    for i in range(CH // 2):
                        second = qq[:, 2 * i * P:2 * (i + 1) * P]
                        mm = pe.matmul(dst[:, i * P:(i + 1) * P].rearrange("p (b m) -> p b m", m=m),
                                       k_first[:, i * P:(i + 1) * P],
                                       second.rearrange("p (b two m) -> p b two m", two=2, m=m)[:, :, 1, :],
                                       start=True, stop=True)
                mm.then_inc(hg_done, 1)

            def keys_token_major(h):
                pe.wait_ge(lvl_ready, 7 * h + 7)
                pe.wait_ge(lvl_taken, 7 * h + 7)
                for c in range(CH - 1):
                    pe.transpose(bank(B_HG)[:, c * P:(c + 1) * P],
                                 kk[:, META + c * P:META + (c + 1) * P], ident[:, :])
                pe.transpose(bank(B_HG)[0:META, (CH - 1) * P:], kk[:, 0:META], ident[:, :]).then_inc(hg_done, 1)

            def values_token_major(vT, b, done):
                for c in range(CH):
                    mm = pe.transpose(bank(b)[:, c * P:(c + 1) * P],
                                      vT[:, META + c * P:META + (c + 1) * P], ident[:, :])
                mm.then_inc(done, 1)

            def state_sums(h):
                pe.wait_ge(va_ready, h + 1)
                g = bank(B_HG)
                for c in range(CH - 1):
                    pe.matmul(g[:, (c + 1) * P:(c + 2) * P], k_tok[:, c, :], v_a[:, c, :], start=True, stop=True)
                pe.matmul(g[:, 0:P], k_tok[0:META, CH - 1, :], v_a[0:META, CH, :], start=True, stop=True) \
                    .then_inc(hg_done, 1)

            def outputs(h):
                pe.wait_ge(st_ready, h + 1)
                for c in range(CH):
                    dst = bank(B_HG)[:, c * P:(c + 1) * P]
                    pe.matmul(dst, aa[:, c, :], v_a[:, c, :], start=True, stop=False)
                    mm = pe.matmul(dst, qq[:, c * P:(c + 1) * P], st[:, c, :], start=False, stop=True)
                mm.then_inc(hg_done, 1)

            def turn(h, branch, b, done):
                pe.wait_ge(on_ready, 2 * h + 1 + branch)
                for c in range(CH):
                    mm = pe.transpose(bank(b)[:, c * P:(c + 1) * P], on[:, c, :], ident[:, :])
                mm.then_inc(done, 1)

            def scores(h, b):
                if b == 0:
                    pe.wait_ge(rope_ready, h + 1)
                else:
                    pe.wait_ge(exp_done, 8 * h + 2 * b)
                if b == CH - 1:
                    pe.wait_ge(pT_ready, 4 * h + b)
                n = n_keys(b)
                at_k = 0 if b < CH - 1 else META
                half = [slice(comp * DA_D, (comp + 1) * DA_D) for comp in range(2)]
                q_b = slice(b * P, (b + 1) * P)

                def meta(comp):
                    return pe.matmul(bank(B_T)[:, comp * META:(comp + 1) * META], qT[half[comp], q_b],
                                     kT[half[comp], 0:META], start=True, stop=True)

                passes = ((qT, kT),) if b == 0 else ((qT_hi, kT_hi), (qT_hi, kT_lo), (qT_lo, kT_hi))
                if b == CH - 1:
                    meta(0).then_inc(meta_scored, 1)
                for i, (q, k) in enumerate(passes):
                    for comp in range(2):
                        pe.matmul(bank(B_S + comp)[:, 0:n - at_k], q[half[comp], q_b], k[half[comp], at_k:n],
                                  start=i == 0, stop=False, skip_group_check=True)
                if b == CH - 1:
                    pe.wait_ge(meta_scored, h + 1)
                    meta(1)
                for comp in range(2):
                    mm = pe.matmul(bank(B_S + comp)[:, n - at_k - P:n - at_k], ident_bf[:, :], bias_bf[:, :],
                                   start=False, stop=True, skip_group_check=True)
                mm.then_inc(at_done, 1)

            def turn_probs(h, b):
                pe.wait_ge(p_ready, 4 * h + b + 1)
                p = e1[:, b % 2, :]
                if b == 0:
                    pe.wait_ge(vb_ready, h + 1)
                    pe.transpose(bank(B_T)[0:META, 256:256 + P], vT_b[:, 0:META], ident[:, :])
                else:
                    pe.wait_ge(pT_ready, 4 * h + b)
                for j in range(b + 1):
                    pe.transpose(bank(B_T)[:, j * P:(j + 1) * P], p[:, META + j * P:META + (j + 1) * P],
                                 ident[:, :])
                dst = bank(B_T if b < CH - 1 else B_A)[0:META, 3 * P:]
                pe.transpose(dst, p[:, 0:META], ident[:, :]).then_inc(at_done, 1)

            def attend(h, b):
                pe.wait_ge(pT_ready, 4 * h + b + 1)
                dst = bank(B_A)[:, b * P:(b + 1) * P]
                for j in range(b + 1):
                    pe.matmul(dst, pT[:, j, :], v_b[:, j, :], start=(j == 0), stop=False)
                pe.matmul(dst, pT[0:META, CH, :], v_b[0:META, CH, :], start=False, stop=True) \
                    .then_inc(at_done, 1)

            def head(h, last):
                for t in range(SECTIONS * KT):
                    p, g = t // KT, t % KT
                    if p < SECTIONS - AHEAD or not last:
                        groups(SECTIONS * h + AHEAD + p, (p + AHEAD) % SECTIONS, p % SLOTS, [g])
                    else:
                        merge_gate(p - 4, [g])
                    for e in range(1, 8):
                        if t == HG_AT[HG_STEPS[e - 1]]:
                            level(h, e)
                    for b in range(2):
                        if t == AT_AT[f"s{b}"]:
                            scores(h, b)
                    if t == HG_AT["keys"]:
                        keys_token_major(h)
                    if t == AT_AT["values"]:
                        pe.wait_ge(sec_taken, SECTIONS * h + 7)
                        pe.wait_ge(og_ready, 2 * h + 2)
                        values_token_major(vT_b, B_T, at_done)
                    if t == HG_AT["values"]:
                        pe.wait_ge(ktok_ready, h + 1)
                        values_token_major(vT_a, B_HG, hg_done)
                    if t == HG_AT["sums"]:
                        state_sums(h)
                    if t == HG_AT["out"]:
                        outputs(h)
                    if t == HG_AT["turn"]:
                        turn(h, 0, B_HG, hg_done)
                    for b in range(CH):
                        if t == AT_AT[f"t{b}"]:
                            turn_probs(h, b)
                        if b >= 2 and t == AT_AT[f"s{b}"]:
                            scores(h, b)
                        if t == AT_AT[f"a{b}"]:
                            attend(h, b)
                    if t == AT_AT["turn"]:
                        turn(h, 1, B_T, at_done)

            with pe.Fori(0, HEADS - 1) as h:
                head(h, False)
            head(HEADS - 1, True)

            def product(u, slot, rhs, dst):
                pe.wait_ge(lo_ready, u + 1)
                for k in range(KT):
                    w = tuple(a[:, slot, k * P:(k + 1) * P] for a in (w_hi, w_lo))
                    last = three(dst, w, tuple(a[:, k, :] for a in rhs), k == 0, k == KT - 1)
                last.then_inc(w_used, 1)

            u_x = tuple(a[:, :, META:TOK] for a in (uT_hi, uT_lo))
            branches = (oa_hi, oa_lo), (ob_hi, ob_lo)
            pe.wait_ge(oglo_ready, 2 * HEADS - 1)
            for d in range(2):
                for j in range(2):
                    if (d, j) == (0, 1):
                        pe.wait_ge(oglo_ready, 2 * HEADS)
                        pe.wait_ge(sec_taken, T0 + 4)
                    product(T0 + 4 + 2 * d + j, 2 * d + j, branches[j], bank(4 + 2 * d + j))
            with pe.Fori(0, KT // 2 - 1) as i:
                for dd in range(2):
                    u = T0 + 8 + 8 * i + 4 * dd
                    for j in range(2):
                        pe.wait_ge(gate_taken, 4 * i + 2 * dd + j + 1)
                        product(u + j, j, u_x, bank(4 * dd + j))
                    for j in range(2):
                        pe.wait_ge(y_taken, 4 * i + 2 * dd + j + 1)
                        product(u + 2 + j, 2 + j, branches[j], bank(4 * dd + 2 + j))
            pe.wait_ge(y_taken, 2 * KT - 2)
            def project(j, c, t):
                for k in range(2):
                    mt = tuple(a[:, 2 * c + k, t * P:(t + 1) * P] for a in (m_hi, m_lo))
                    ws = tuple(a[:, c, 512 * k:512 * (k + 1)] for a in (w_hi, w_lo))
                    last = three(bank(4 * j + t), mt, ws, c == 0 and k == 0, c == 3 and k == 1)
                return last

            for c in range(4):
                pe.wait_ge(lo_ready, O0 + c + 1)
                pe.wait_ge(mlo_ready, 2 * c + 2)
                for t in range(CH):
                    last = project(0, c, t)
                    if c == 3 and t < CH - 1:
                        last.then_inc(o_done, 1)
                last.then_inc(w_used, 1)
            pe.wait_ge(y_taken, 2 * KT)
            for t in range(CH):
                for c in range(4):
                    if t == 0:
                        pe.wait_ge(lo_ready, O0 + 4 + c + 1)
                    last = project(1, c, t)
                last.then_inc(o_done, 1)

        @block.scalar
        def _(act):
            act.dma_start(ident[:, :], c_ident).then_inc(ident_in, 16)
            act.dma_start(g_in[:, :], norm_g.to_broadcast([P, D])).then_inc(norm_in, 16)
            act.dma_start(x_in[0:META, CH, :], meta_tokens).then_inc(meta_in, 16)
            act.wait_ge(g_pre, 1)
            act.activation(warm, half_neg, ACT.Square)
            act.sem_inc(og_ready, 2)
            act.sem_inc(hg_done, HG)
            act.sem_inc(at_done, AT)
            act.sem_inc(gate_ready, 2)
            act.sem_inc(oghi_ready, 2)
            act.sem_inc(gate_taken, 4)

            def square_x(n):
                i = X_ORDER[n]
                m = P if i < CH else META
                act.wait_ge(*((x_loaded[i], 16) if i < CH else (meta_in, 16)))
                if n > 0:
                    act.wait_ge(x_squared, n)
                act.activation(x_sq[0:m, :], x_in[0:m, i, :], ACT.Square, accum_out=ss[0:m, i:i + 1]) \
                    .then_inc(x_squared, 1)

            def turned_x(n):
                i = X_ORDER[n]
                act.wait_ge(x_turned, n + 1)
                if i == CH:
                    act.activation(uT_hi[:, :, 0:META], bank(3)[:, 0:KT * META].rearrange("p (k t) -> p k t", k=KT),
                                   ACT.Copy).then_inc(u_ready_hi, 1)
                    return
                for g in range(2):
                    ins = act.activation(uT_hi[:, 4 * g:4 * g + 4, META + i * P:META + (i + 1) * P],
                                         bank(4 + 2 * (i % 2) + g).rearrange("p (k t) -> p k t", k=4), ACT.Copy)
                ins.then_inc(u_ready_hi, 1)

            square_x(0)
            square_x(1)
            square_x(2)
            turned_x(0)
            square_x(3)
            turned_x(1)
            convert_hi(act, 0, 0, 1)
            turned_x(2)
            square_x(4)
            turned_x(3)
            convert_hi(act, 1, 1, 1)
            turned_x(4)
            convert_hi(act, 2, 2, 2)
            act.wait_ge(v_pre, 4)
            act.activation(lam2, lam2, ACT.Exp).then_inc(a_pre, 1)
            act.wait_ge(v_pre, 7)
            act.activation(e_0, e_0, ACT.Exp).then_inc(a_pre, 1)
            act.activation(e_1, e_1, ACT.Exp).then_inc(a_pre, 1)

            def take(h, s):
                act.wait_ge(w_used, SECTIONS * h + s + 1)
                pair = lambda t: t.rearrange("p (b t) -> p b t", b=2)
                if s == 0:
                    act.wait_ge(hg_done, hg(h - 1, "keys"))
                    act.activation(pair(kk[:, :]), PAIR, ACT.Tanh, scale=0.5).then_inc(sec_taken, 1)
                elif s == 1:
                    act.wait_ge(hg_done, hg(h - 1, "l2"))
                    act.activation(q_1[:, :, 0:P], bank(2).rearrange("p (c t) -> p c t", c=CH), ACT.Copy) \
                        .then_inc(sec_taken, 1)
                elif s == 2:
                    act.wait_ge(at_done, atn(h - 1, "s3"))
                    act.activation(pair(kT[:, :]), PAIR, ACT.Copy).then_inc(sec_taken, 1)
                elif s == 3:
                    act.wait_ge(at_done, atn(h - 1, "s3"))
                    act.activation(qT[:, :], bank(2), ACT.Copy).then_inc(sec_taken, 1)
                elif s == 4:
                    act.wait_ge(hg_done, hg(h - 1, "values"))
                    act.activation(pair(vT_a[:, :]), PAIR, ACT.Copy).then_inc(sec_taken, 1)
                elif s == 6:
                    act.wait_ge(at_done, atn(h - 1, "t0"))
                    act.activation(pair(vT_b[:, :]), PAIR, ACT.Copy).then_inc(sec_taken, 1)
                else:
                    act.wait_ge(gate_ready, 2 * h + (2 if s == 5 else 3))
                    act.activation(th_z[:, :], bank(2), ACT.Tanh, scale=0.5)
                    act.activation(z_g[:, :], bank(2), ACT.Copy, scale=(gain_a if s == 5 else gain_b)) \
                        .then_inc(sec_taken, 1)

            for n in range(AHEAD):
                if n > 0:
                    take(0, n - 1)
                convert_hi(act, n + 3, (n + 3) % SLOTS, (n + 3) // RAW + 1)

            def square(h, branch, b, done, step):
                act.wait_ge(done, step)
                act.activation(sq[:, :, :].rearrange("p c d -> p (c d)"), bank(b), ACT.Square) \
                    .then_inc(o_squared, 1)

            def exps(h, b):
                act.wait_ge(nb_ready, 4 * h + b + 1)
                act.wait_ge(at_done, atn(h - 1, f"t{b + 2}") if b < 2 else atn(h, f"t{b - 2}"))
                n = n_keys(b)
                for comp in range(2):
                    e = (e1, e2)[comp][:, b % 2, :]
                    if b < CH - 1:
                        ins = act.activation(e[:, 0:n], bank(B_S + comp)[:, 0:n], ACT.Exp, bias=nb[:, comp:comp + 1],
                                             scale=SCALE, accum_out=lsum[:, comp:comp + 1])
                    else:
                        act.activation(e[:, 0:META], bank(B_T)[:, comp * META:(comp + 1) * META], ACT.Exp,
                                       bias=nb[:, comp:comp + 1], scale=SCALE, accum_out=lsum2[:, comp:comp + 1])
                        ins = act.activation(e[:, META:n], bank(B_S + comp), ACT.Exp, bias=nb[:, comp:comp + 1],
                                             scale=SCALE, accum_out=lsum[:, comp:comp + 1])
                    ins.then_inc(exp_done, 1)

            def probs_out(h, b):
                act.wait_ge(at_done, atn(h, f"t{b}"))
                if b == 0:
                    act.activation(v_b[0:META, CH, :], bank(B_T)[0:META, 256:256 + P], ACT.Copy)
                act.activation(pT[:, 0:b + 1, :].rearrange("p j q -> p (j q)"), bank(B_T)[:, 0:(b + 1) * P], ACT.Copy)
                act.activation(pT[0:META, CH, :], bank(B_T if b < CH - 1 else B_A)[0:META, 3 * P:], ACT.Copy) \
                    .then_inc(pT_ready, 1)

            def values_out(h, b, v, done, step, ready):
                act.wait_ge(done, step)
                act.activation(v[:, 0:CH, :].rearrange("p c d -> p (c d)"), bank(b), ACT.Copy).then_inc(ready, 1)

            def rotated_hi(h, n):
                act.wait_ge(rotated, 2 * h + n + 1)
                act.activation((kT_hi, qT_hi)[n][:, :], (kT, qT)[n][:, :], ACT.Copy).then_inc(rothi_ready, 1)

            def split_hi(h, branch):
                act.wait_ge(og_ready, 2 * h + 3 + branch)
                act.activation((oa_hi, ob_hi)[branch][:, bass.ds(h, 1), :].rearrange("p a t -> p (a t)"),
                               og[:, :], ACT.Copy).then_inc(oghi_ready, 1)

            def head(h, last):
                def period(p):
                    if p == 0:
                        take(h, 3)
                    elif p <= SECTIONS - AHEAD:
                        take(h, p + 3)
                    elif not last:
                        take(h + 1, p - 5)
                    else:
                        gate_out(p - 5)

                def conv(p):
                    convert_hi(act, SECTIONS * h + 7 + p, (7 + p) % SLOTS, SECTIONS // RAW * h + (7 + p) // RAW + 1)

                period(0)
                rotated_hi(h, 0)
                period(1)
                period(2)
                rotated_hi(h, 1)
                conv(0)
                exps(h, 0)
                period(3)
                conv(1)
                act.wait_ge(hg_done, hg(h, "keys"))
                act.activation(k_tok[:, 0:CH - 1, :].rearrange("p c d -> p (c d)"), bank(B_HG)[:, 0:(CH - 1) * P],
                               ACT.Copy)
                act.activation(k_tok[0:META, CH - 1, :], bank(B_HG)[0:META, (CH - 1) * P:], ACT.Copy) \
                    .then_inc(ktok_ready, 1)
                exps(h, 1)
                values_out(h, B_T, v_b, at_done, atn(h, "values"), vb_ready)
                values_out(h, B_HG, v_a, hg_done, hg(h, "values"), va_ready)
                probs_out(h, 0)
                period(4)
                conv(2)
                exps(h, 2)
                square(h, 0, B_HG, hg_done, hg(h, "out"))
                conv(3)
                probs_out(h, 1)
                period(5)
                conv(4)
                probs_out(h, 2)
                split_hi(h, 0)
                exps(h, 3)
                conv(5)
                period(6)
                conv(6)
                probs_out(h, 3)
                square(h, 1, B_A, at_done, atn(h, "a3"))
                period(7)
                conv(7)
                split_hi(h, 1)

            def gate_out(i):
                act.wait_ge(w_used, T0 + i + 1)
                if i == 0:
                    act.wait_ge(on_ready, 2 * HEADS - 1)
                act.activation(tg[:, i, :], bank(0 if i % 2 == 0 else 2), ACT.Tanh, scale=0.5) \
                    .then_inc(sec_taken, 1)

            with act.Fori(0, HEADS - 1) as h:
                head(h, False)
            head(HEADS - 1, True)
            gate_out(3)

            def merge_hi(d):
                act.wait_ge(m_sum, d + 1)
                act.activation(m_hi[:, bass.ds(d, 1), :].rearrange("p a t -> p (a t)"), t_m[:, 0, :], ACT.Copy,
                               scale=0.5).then_inc(mhi_ready, 1)

            def ahead(u, at_u, loads):
                convert_hi(act, u, at_u % SLOTS, loads)

            for u in range(T0 + 7, T0 + 9):
                ahead(u, u, u // RAW + 1)
            merge_hi(0)
            for u in range(T0 + 9, T0 + 11):
                ahead(u, u, u // RAW + 1)
            merge_hi(1)
            with act.Fori(0, KT // 2 - 1) as i:
                for dd in range(2):
                    for j in range(4):
                        at_u = T0 + 11 + 4 * dd + j
                        ahead(8 * i + at_u, at_u, 8 // RAW * i + at_u // RAW + 1)
                        if j in (1, 2):
                            g = j - 1
                            act.wait_ge(w_used, T0 + 8 * i + 8 + 4 * dd + g + 1)
                            act.wait_ge(y_taken, 4 * i + 2 * dd + 2 + g + 1)
                            act.activation(t_gate[:, g, :], bank(4 * dd + g), ACT.Tanh, scale=0.5) \
                                .then_inc(gate_taken, 1)
                    merge_hi(2 * i + 2 + dd)
            for u in range(O0 + 3, ALL_UNITS):
                ahead(u, u, u // RAW + 1)
            def square_out(j, t):
                act.wait_ge(o_taken, CH * j + t + 1)
                if j + t > 0:
                    act.wait_ge(o_sq, CH * j + t)
                act.activation(y_sq[:, :], y_out[:, t, 512 * j:512 * (j + 1)], ACT.Square,
                               accum_out=(ss, ss2)[j][:, t:t + 1]).then_inc(o_sq, 1)

            def finish_left(t):
                act.wait_ge(o_gained, t + 1)
                act.wait_ge(o_rstd, t + 1)
                act.activation(y_out[:, t, 0:512], y_out[:, t, 0:512], ACT.Copy, scale=rstd[:, t:t + 1]) \
                    .then_inc(y_left, 1)

            for t in range(CH):
                square_out(0, t)
            for t in range(CH):
                square_out(1, t)
                finish_left(t)

        @block.vector
        def _(dve):
            own = [0]

            def pre(ins):
                own[0] += 1
                ins.then_inc(v_pre, 1)
                return own[0]

            def norm_x(n):
                i = X_ORDER[n]
                m = P if i < CH else META
                dve.wait_ge(x_rstd, n + 1)
                if n == 0:
                    dve.wait_ge(norm_in, 16)
                dve.scalar_tensor_tensor(x_in[0:m, i, :], x_in[0:m, i, :], rstd[0:m, i:i + 1], g_in[0:m, :],
                                         ALU.mult, ALU.mult).then_inc(x_normed, 1)

            def mean_x(n):
                i = X_ORDER[n]
                m = P if i < CH else META
                dve.wait_ge(x_squared, n + 1)
                dve.tensor_scalar(ms[0:m, i:i + 1], ss[0:m, i:i + 1], 1.0 / D, EPS, ALU.mult, ALU.add) \
                    .then_inc(x_ms, 1)

            def turned_x(n):
                i = X_ORDER[n]
                dve.wait_ge(u_ready_hi, n + 1)
                if i == CH:
                    dve.tensor_tensor(uT_lo[:, :, 0:META], bank(3)[:, 0:KT * META].rearrange("p (k t) -> p k t", k=KT),
                                      uT_hi[:, :, 0:META].bitcast(F32), ALU.subtract).then_inc(u_ready_lo, 1)
                    return
                for g in range(2):
                    lo, hi = (a[:, 4 * g:4 * g + 4, META + i * P:META + (i + 1) * P] for a in (uT_lo, uT_hi))
                    ins = dve.tensor_tensor(lo, bank(4 + 2 * (i % 2) + g).rearrange("p (k t) -> p k t", k=4),
                                            hi.bitcast(F32), ALU.subtract)
                ins.then_inc(u_ready_lo, 1)

            mean_x(0)
            mean_x(1)
            norm_x(0)
            norm_x(1)
            mean_x(2)
            norm_x(2)
            turned_x(0)
            mean_x(3)
            dve.wait_ge(pe_pre, 1)
            pre(dve.tensor_copy(lbt, bank(3)[:, 256:256 + 2 * HEADS + 2]))
            turned_x(1)
            norm_x(3)
            convert_lo(dve, 0, 0)
            turned_x(2)
            mean_x(4)
            norm_x(4)
            turned_x(3)
            convert_lo(dve, 1, 1)
            turned_x(4)
            convert_lo(dve, 2, 2)
            dve.wait_ge(tables_in, 64)
            pre(dve.tensor_copy(bias_bf[:, :], bias_in[:, :]))
            pre(dve.tensor_tensor(lam_pr[:, :, :], lam_in[:, 0:4:2, :], lam_in[:, 1:4:2, :], ALU.mult))
            dve.wait_ge(v_pre, 3)
            pre(dve.tensor_reduce(lam2, lam_pr[:, :, :], AX.X, ALU.add))
            pre(dve.tensor_tensor(e_m, lbt[:, 0:HEADS], lbt[:, HEADS:2 * HEADS], ALU.max))
            dve.wait_ge(v_pre, 5)
            pre(dve.tensor_tensor(e_0, lbt[:, 0:HEADS], e_m, ALU.subtract))
            pre(dve.tensor_tensor(e_1, lbt[:, HEADS:2 * HEADS], e_m, ALU.subtract))
            pre(dve.tensor_copy(ident_bf[:, :], ident[:, :]))
            pre(dve.tensor_scalar(gain_a, lbt[:, 2 * HEADS:2 * HEADS + 1], 0.5, None, ALU.mult))
            pre(dve.tensor_scalar(gain_b, lbt[:, 2 * HEADS + 1:2 * HEADS + 2], 0.5 * (1.0 - LAM_INIT), None, ALU.mult))
            dve.wait_ge(a_pre, 1)
            n = pre(dve.tensor_tensor(neg_lam, lam2[:, 1:2], lam2[:, 0:1], ALU.subtract))
            dve.wait_ge(v_pre, n)
            pre(dve.tensor_scalar(neg_lam, neg_lam, LAM_INIT, None, ALU.subtract))
            dve.wait_ge(a_pre, 3)
            n = pre(dve.tensor_tensor(e_1, e_0, e_1, ALU.add))
            dve.wait_ge(v_pre, n)
            n = pre(dve.reciprocal(e_m, e_1))
            dve.wait_ge(v_pre, n)
            n = pre(dve.tensor_tensor(e_1, e_0, e_m, ALU.mult))
            dve.wait_ge(v_pre, n)
            pre(dve.tensor_scalar(f_mul, e_1, -0.5, 0.5, ALU.mult, ALU.add))
            n = pre(dve.tensor_scalar(f_neg, e_1, 0.5, -0.5, ALU.mult, ALU.add))
            dve.wait_ge(v_pre, n)
            n = pre(dve.tensor_tensor(f_add, e_1, f_mul, ALU.add))
            dve.wait_ge(v_pre, n)
            for n in range(AHEAD):
                convert_lo(dve, n + 3, (n + 3) % SLOTS)

            t_of, at_ = {1: f[:, :]}, 0
            for m in (2, 4, 8, 16, 32, 64, 128):
                n = TOK // m if m <= META else SEQ // m
                t_of[m] = tt[:, at_:at_ + n]
                at_ += n
            OWN = 52

            def head(h):
                count = [0]

                def chained():
                    dve.wait_ge(dve_own, OWN * h + count[0])

                def mark(ins):
                    count[0] += 1
                    ins.then_inc(dve_own, 1)

                def chain(ins):
                    mark(ins)
                    chained()

                def conv(p):
                    convert_lo(dve, SECTIONS * h + 7 + p, (7 + p) % SLOTS)

                def gate(branch):
                    dve.wait_ge(sec_taken, SECTIONS * h + 6 + 2 * branch)
                    dve.scalar_tensor_tensor((gate_a, gate_b)[branch][:, :], th_z[:, :], 1.0, z_g[:, :], ALU.add,
                                             ALU.mult).then_inc(gate_ready, 1)

                first_products = ps[:, B_HG:B_HG + 2, 0:384].rearrange("p b (c t) -> p b c t", c=2)

                def next_level(m):
                    chained()
                    if m > 1:
                        dve.wait_ge(lvl_taken, 7 * h + LEVELS.index(m))
                    dve.wait_ge(hg_done, hg(h, f"l{m}"))
                    if m < META:
                        kv = kk[:, :].rearrange("p (b two m) -> p b two m", two=2, m=m)
                        tk = t_of[m].rearrange("p (b two) -> p b two", two=2)
                        tq = tk[:, META // (2 * m):, :]
                    else:
                        kv = kk[:, META:].rearrange("p (b two m) -> p b two m", two=2, m=m)
                        t = t_of[m][:, 1:] if m == META else t_of[m]
                        tk = tq = t.rearrange("p (b two) -> p b two", two=2)
                    qv = qq[:, :].rearrange("p (b two m) -> p b two m", two=2, m=m)
                    nk, nq = kv.shape[1], qv.shape[1]
                    beside = m in (16, 32)
                    ins = dve.tensor_tensor(kv[:, :, 0, :], kv[:, :, 0, :],
                                            tk[:, :, 1:2].to_broadcast([P, nk, m]), ALU.mult)
                    if beside:
                        mark(ins)
                    ins = dve.tensor_tensor(qv[:, :, 1, :], qv[:, :, 1, :],
                                            tq[:, :, 0:1].to_broadcast([P, nq, m]), ALU.mult)
                    if beside:
                        chained()
                        ins = dve.tensor_copy(
                            k_first.rearrange("p (b m) -> p b m", m=2 * m),
                            kk[:, META:].rearrange("p (b two m) -> p b two m", two=2, m=2 * m)[:, :, 0, :])
                    ins.then_inc(lvl_ready, 1)
                    if m == 1:
                        for b in range(2):
                            ins = dve.tensor_tensor(
                                aa[:, 2 * b:2 * b + 2, :], first_products[:, b, :, 0:P],
                                ident[:, :].rearrange("p (a t) -> p a t", a=1).to_broadcast([P, 2, P]), ALU.mult)
                        chain(ins)
                    mark(dve.tensor_tensor(t_of[2 * m], tk[:, :, 0], tk[:, :, 1], ALU.mult))

                def take_level(e):
                    src = bank(level_bank(e))
                    m = LEVELS[e - 1]
                    if e <= MASKED:
                        for c in range(CH):
                            dst = aa[:, c, :].rearrange("p (b two m) -> p b two m", two=2, m=m)[:, :, 1, :]
                            got = src[:, c * 64:(c + 1) * 64] if e > 1 else first_products[:, c // 2, c % 2, P:]
                            ins = dve.copy_predicated(dst, masks[:, e - 1, :].rearrange("p (b m) -> p b m", m=m),
                                                      got.rearrange("p (b m) -> p b m", m=m))
                        ins.then_inc(lvl_taken, 1)
                        return
                    if m == 64:
                        dve.tensor_copy(v_a[0:META, CH, :], src[0:META, 256:256 + P])
                    for j in range(P // m):
                        c, s = divmod(2 * m * j, P)
                        ins = dve.tensor_copy(
                            aa[s:s + m, c:CH:2, s + m:s + 2 * m],
                            src[j * m:(j + 1) * m, 0:2 * P].rearrange("p (i t) -> p i t", i=2)[:, :, j * m:(j + 1) * m])
                    ins.then_inc(lvl_taken, 1)

                def step_level(e):
                    next_level(LEVELS[e - 1])
                    take_level(e)

                def norm(branch, b):
                    dve.wait_ge(o_squared, 2 * h + branch + 1)
                    chain(dve.tensor_reduce(ss[:, 0:CH], sq[:, :, :], AX.X, ALU.add))
                    dve.tensor_scalar(ms[:, 0:CH], ss[:, 0:CH], 1.0 / P, EPS, ALU.mult, ALU.add) \
                        .then_inc(ms_ready, 1)
                    dve.wait_ge(rstd_ready, 2 * h + branch + 1)
                    r = rstd[:, 0:CH].rearrange("p (c a) -> p c a", a=1).to_broadcast([P, CH, P])
                    dve.tensor_tensor(on[:, :, :], bank(b).rearrange("p (c d) -> p c d", c=CH), r,
                                      ALU.mult).then_inc(on_ready, 1)

                def gated(branch):
                    dve.wait_ge(*((hg_done, hg(h, "turn")) if branch == 0 else (at_done, atn(h, "turn"))))
                    dve.wait_ge(oghi_ready, 2 * h + branch + 2)
                    dve.tensor_tensor(og[:, :], bank((B_HG, B_T)[branch]), (gate_a, gate_b)[branch][:, :], ALU.mult) \
                        .then_inc(og_ready, 1)

                def split_lo(branch):
                    hi, lo = ((oa_hi, oa_lo), (ob_hi, ob_lo))[branch]
                    dve.wait_ge(oghi_ready, 2 * h + branch + 3)
                    at_h = bass.ds(h, 1)
                    dve.tensor_tensor(lo[:, at_h, :].rearrange("p a t -> p (a t)"), og[:, :],
                                      hi[:, at_h, :].rearrange("p a t -> p (a t)").bitcast(F32), ALU.subtract) \
                        .then_inc(oglo_ready, 1)

                def swap_pairs(t):
                    swap = [i + 8 if i < 8 else i - 8 if i < 16 else i for i in range(32)]
                    mark(dve.stream_shuffle(shuf[:, 0:t.shape[1]], t, swap))

                def turn_pairs(t, lo):
                    n = t.shape[1]
                    chained()
                    dve.tensor_tensor(t, t, rope[:, 0, lo:lo + n], ALU.mult)
                    mark(dve.tensor_tensor(shuf[:, 0:n], shuf[:, 0:n], rope[:, 1, lo:lo + n], ALU.mult))

                def add_pairs(t):
                    chained()
                    return dve.tensor_tensor(t, t, shuf[:, 0:t.shape[1]], ALU.add)

                def rotated_lo(n):
                    dve.wait_ge(rothi_ready, 2 * h + n + 1)
                    return dve.tensor_tensor((kT_lo, qT_lo)[n][:, :], (kT, qT)[n][:, :],
                                             (kT_hi, qT_hi)[n][:, :].bitcast(F32), ALU.subtract)

                def row_max(b):
                    n = min(n_keys(b), 512)
                    dve.wait_ge(at_done, atn(h, f"s{b}"))
                    if b == CH - 1:
                        dve.tensor_reduce(mx2, bank(B_T)[:, 0:2 * META].rearrange("p (c n) -> p c n", c=2), AX.X,
                                          ALU.max)
                    chain(dve.tensor_reduce(mx, ps[:, B_S:B_S + 2, 0:n], AX.X, ALU.max))
                    if b == CH - 1:
                        chain(dve.tensor_tensor(mx, mx, mx2, ALU.max))
                    dve.tensor_scalar(nb, mx, -SCALE, None, ALU.mult).then_inc(nb_ready, 1)

                def probs(b):
                    n = n_keys(b)
                    a1, a2 = e1[:, b % 2, 0:n], e2[:, b % 2, 0:n]
                    dve.wait_ge(exp_done, 8 * h + 2 * b + 2)
                    if b == CH - 1:
                        chain(dve.tensor_tensor(lsum, lsum, lsum2, ALU.add))
                    chain(dve.reciprocal(rl, lsum))
                    dve.tensor_tensor(rl[:, 1:2], rl[:, 1:2], neg_lam, ALU.mult)
                    chain(dve.tensor_scalar(a1, a1, rl[:, 0:1], None, ALU.mult))
                    dve.scalar_tensor_tensor(a1, a2, rl[:, 1:2], a1, ALU.mult, ALU.add).then_inc(p_ready, 1)

                hcol = bass.ds(h, 1)
                dve.wait_ge(sec_taken, SECTIONS * h + 2)
                dve.wait_ge(hg_done, hg(h - 1, "out"))
                dve.tensor_scalar(f[:, :], kk[:, :], f_mul[:, hcol], f_add[:, hcol], ALU.mult, ALU.add)
                chain(dve.tensor_scalar(kk[:, :], kk[:, :], f_neg[:, hcol], f_mul[:, hcol], ALU.mult, ALU.add))
                odd = q_1[:, :, 0:P].rearrange("p c (b two) -> p c b two", two=2)[:, :, :, 1]
                dve.tensor_tensor(q_1[:, :, P:], odd,
                                  f[:, META:].rearrange("p (c b two) -> p c b two", c=CH, two=2)[:, :, :, 1],
                                  ALU.mult).then_inc(k_ready, 1)
                dve.wait_ge(sec_taken, SECTIONS * h + 3)
                mark(dve.tensor_tensor(qq[:, :].rearrange("p (c t) -> p c t", c=CH), q_1[:, :, 0:P],
                                       f[:, META:].rearrange("p (c t) -> p c t", c=CH), ALU.mult))
                swap_pairs(kT[:, :])
                turn_pairs(kT[:, :], 0)
                dve.wait_ge(sec_taken, SECTIONS * h + 4)
                step_level(1)
                add_pairs(kT[:, :]).then_inc(rotated, 1)
                step_level(2)
                rotated_lo(0)
                swap_pairs(qT[:, :])
                step_level(3)
                turn_pairs(qT[:, :], META)
                step_level(4)
                add_pairs(qT[:, :]).then_inc(rotated, 1)
                step_level(5)
                rotated_lo(1).then_inc(rope_ready, 1)
                step_level(6)
                conv(0)
                row_max(0)
                step_level(7)
                probs(0)
                conv(1)
                row_max(1)
                probs(1)
                gate(0)
                dve.wait_ge(hg_done, hg(h, "sums"))
                chain(dve.tensor_copy(st[:, 0, :], bank(B_HG)[:, 0:P]))
                for c in range(CH - 1):
                    ins = dve.scalar_tensor_tensor(st[:, c + 1, :], st[:, c, :], t_of[128][:, c:c + 1],
                                                   bank(B_HG)[:, (c + 1) * P:(c + 2) * P], ALU.mult, ALU.add)
                    if c < CH - 2:
                        chain(ins)
                    else:
                        ins.then_inc(st_ready, 1)
                row_max(2)
                conv(2)
                norm(0, B_HG)
                conv(3)
                probs(2)
                gated(0)
                conv(4)
                gate(1)
                row_max(3)
                split_lo(0)
                probs(3)
                conv(5)
                conv(6)
                norm(1, B_A)
                conv(7)
                gated(1)
                split_lo(1)
                assert count[0] <= OWN, count
                if count[0] < OWN:
                    dve.sem_inc(dve_own, OWN - count[0])

            with dve.Fori(0, HEADS - 1) as h:
                head(h)
            head(HEADS - 1)

            def merge(d, last_u, gates, banks):
                dve.wait_ge(mlo_ready, d) if not isinstance(d, int) or d > 0 else None
                for b in range(2):
                    dve.wait_ge(w_used, last_u + b)
                    dve.scalar_tensor_tensor(t_m[:, b, :], gates[:, b, :], 1.0, bank(banks + b),
                                             ALU.add, ALU.mult).then_inc(y_taken, 1)
                dve.wait_ge(y_taken, 2 * d + 2)
                dve.tensor_tensor(t_m[:, 0, :], t_m[:, 0, :], t_m[:, 1, :], ALU.add).then_inc(m_sum, 1)

            def merge_lo(d):
                dve.wait_ge(mhi_ready, d + 1)
                at_d = bass.ds(d, 1)
                dve.scalar_tensor_tensor(m_lo[:, at_d, :].rearrange("p a t -> p (a t)"), t_m[:, 0, :], 0.5,
                                         m_hi[:, at_d, :].rearrange("p a t -> p (a t)").bitcast(F32),
                                         ALU.mult, ALU.subtract).then_inc(mlo_ready, 1)

            convert_lo(dve, T0 + 7, (T0 + 7) % SLOTS)
            convert_lo(dve, T0 + 8, (T0 + 8) % SLOTS)
            merge(0, T0 + 5, tg[:, 0:2, :], 4)
            convert_lo(dve, T0 + 9, (T0 + 9) % SLOTS)
            merge_lo(0)
            convert_lo(dve, T0 + 10, (T0 + 10) % SLOTS)
            merge(1, T0 + 7, tg[:, 2:4, :], 6)
            merge_lo(1)
            with dve.Fori(0, KT // 2 - 1) as i:
                for dd in range(2):
                    for j in range(4):
                        at_u = T0 + 11 + 4 * dd + j
                        convert_lo(dve, 8 * i + at_u, at_u % SLOTS)
                    dve.wait_ge(gate_taken, 4 * i + 2 * dd + 6)
                    merge(2 * i + 2 + dd, T0 + 8 * i + 8 + 4 * dd + 3, t_gate, 4 * dd + 2)
                    merge_lo(2 * i + 2 + dd)
            for u in range(O0 + 3, ALL_UNITS):
                convert_lo(dve, u, u % SLOTS)
            dve.wait_ge(xres_loaded, 16 * (CH + 1))
            def add_x(j, t):
                if (j, t) == (0, CH - 1):
                    dve.wait_ge(w_used, O0 + 4)
                else:
                    dve.wait_ge(o_done, t + 1 if j == 0 else CH + t)
                dve.tensor_tensor(y_out[:, t, 512 * j:512 * (j + 1)], bank(4 * j + t),
                                  x_res[:, t, 512 * j:512 * (j + 1)], ALU.add).then_inc(o_taken, 1)
            def gain_left(t):
                dve.wait_ge(o_sq, t + 1)
                dve.tensor_scalar(ss[:, t:t + 1], ss[:, t:t + 1], 1.0 / D, EPS, ALU.mult, ALU.add) \
                    .then_inc(o_half, 1)
                dve.tensor_tensor(y_out[:, t, 0:512], y_out[:, t, 0:512], g_fin[:, 0:512], ALU.mult) \
                    .then_inc(o_gained, 1)

            def mean(t):
                dve.wait_ge(o_half, t + 1)
                dve.wait_ge(o_sq, CH + t + 1)
                dve.scalar_tensor_tensor(ms[:, t:t + 1], ss2[:, t:t + 1], 1.0 / D, ss[:, t:t + 1], ALU.mult,
                                         ALU.add).then_inc(o_ms, 1)

            def finish_right(t):
                dve.wait_ge(o_rstd, t + 1)
                dve.scalar_tensor_tensor(y_out[:, t, 512:], y_out[:, t, 512:], rstd[:, t:t + 1], g_fin[:, 512:],
                                         ALU.mult, ALU.mult).then_inc(y_right, 1)

            for t in range(CH):
                add_x(0, t)
            for t in range(CH):
                gain_left(t)
            for t in range(CH):
                add_x(1, t)
                mean(t)
                finish_right(t)


_INS = ["x", "meta_tokens", "norm_g", "w_in", "hg_lb_logits", "hg_norm_g", "da_lambda", "da_norm_g",
        "w_branch_a", "w_branch_b", "w_out", "final_g"]


def kernel(**inputs):
    import concourse.bacc as bacc
    from concourse.bass_utils import run_bass_kernel_spmd as run

    nc = bacc.Bacc("TRN2", target_bir_lowering=False, num_devices=1)
    arrays, args = {}, []
    laid = {n: np.ascontiguousarray(inputs[n]) for n in _INS}
    laid.update(constants())
    for name, a in laid.items():
        arrays[f"in_{name}"] = a
        args.append(nc.dram_tensor(f"in_{name}", a.shape, mybir.dt.from_np(a.dtype), kind="ExternalInput").ap())
    args.append(nc.dram_tensor("out_0", (1, SEQ, D), F32, kind="ExternalOutput").ap())
    build(nc, *args)
    r = run(nc, [arrays], core_ids=[0])
    return r.results[0]["out_0"]
```
